# Optimizing a Trainium2 kernel written in Bass

```python
import jax, jax.numpy as jnp
from jax import lax
import numpy as np

D_MODEL = 1024
BATCH = 1
SEQ = 512
DEPTH = 2

SC_WIDTH = D_MODEL // 2
SC_KERNEL = 3
MLA_HEADS = 8
MLA_NOPE = 64
MLA_ROPE = 32
MLA_V = 64
MLA_Q_RANK = 384
MLA_KV_RANK = 256
ROPE_BASE = 10000.0
Q_BLOCK = 128
IN_COLS = 3 * SC_WIDTH + MLA_Q_RANK + MLA_KV_RANK + MLA_ROPE
MIX_WIDTH = SC_WIDTH + MLA_HEADS * MLA_V
CONF_KERNEL = 31
CONF_WIDTH = D_MODEL
D_FF = 4 * D_MODEL
N_EVEN = (DEPTH + 1) // 2
N_ODD = DEPTH // 2
EPS = 1e-6


def rms_norm(x, g):
    xf = x.astype(jnp.float32)
    y = xf * lax.rsqrt(jnp.mean(xf * xf, axis=-1, keepdims=True) + EPS)
    return (y * g.astype(jnp.float32)).astype(x.dtype)

def layer_norm(x, g, b):
    xf = x.astype(jnp.float32)
    mu = jnp.mean(xf, axis=-1, keepdims=True)
    var = jnp.mean(jnp.square(xf - mu), axis=-1, keepdims=True)
    y = (xf - mu) * lax.rsqrt(var + EPS)
    return (y * g.astype(jnp.float32) + b.astype(jnp.float32)).astype(x.dtype)

def depthwise_conv(x, w):
    k = w.shape[0]
    return lax.conv_general_dilated(
        x, w[:, None, :].astype(x.dtype), window_strides=(1,),
        padding=[(k // 2, k // 2)], dimension_numbers=('NWC', 'WIO', 'NWC'),
        feature_group_count=x.shape[-1])

def apply_rope(x, cos, sin):
    half = x.shape[-1] // 2
    xf = x.astype(jnp.float32)
    x1, x2 = xf[..., :half], xf[..., half:]
    out = jnp.concatenate([x1 * cos - x2 * sin, x2 * cos + x1 * sin], axis=-1)
    return out.astype(x.dtype)

def block_attention(q, k, v):
    b, s, h, dq = q.shape
    nblk = s // Q_BLOCK
    qb = q.reshape(b, nblk, Q_BLOCK, h, dq).transpose(1, 0, 2, 3, 4)
    kf = k.astype(jnp.float32)
    scale = dq ** -0.5

    def one_block(q_blk):
        sc = jnp.einsum('bqhd,bkhd->bhqk', q_blk.astype(jnp.float32), kf) * scale
        p = jax.nn.softmax(sc, axis=-1)
        return jnp.einsum('bhqk,bkhd->bqhd', p.astype(v.dtype), v)

    o = lax.map(one_block, qb)
    return o.transpose(1, 0, 2, 3, 4).reshape(b, s, h * v.shape[-1])

def parallel_conv_mla(h, positions, w_in, sc_kernel, q_norm, w_uq, kv_norm, w_ukv, w_out):
    b, s, _ = h.shape
    proj = h @ w_in
    cuts = [SC_WIDTH, 2 * SC_WIDTH, 3 * SC_WIDTH,
            3 * SC_WIDTH + MLA_Q_RANK, 3 * SC_WIDTH + MLA_Q_RANK + MLA_KV_RANK]
    gate_b, gate_c, xs, q_lat, kv_lat, k_rope = jnp.split(proj, cuts, axis=-1)

    y_a = gate_b * depthwise_conv(gate_c * xs, sc_kernel)

    q = (rms_norm(q_lat, q_norm) @ w_uq).reshape(b, s, MLA_HEADS, MLA_NOPE + MLA_ROPE)
    q_nope, q_pe = q[..., :MLA_NOPE], q[..., MLA_NOPE:]
    kv = (rms_norm(kv_lat, kv_norm) @ w_ukv).reshape(b, s, MLA_HEADS, MLA_NOPE + MLA_V)
    k_nope, v = kv[..., :MLA_NOPE], kv[..., MLA_NOPE:]
    half = MLA_ROPE // 2
    inv_freq = 1.0 / (ROPE_BASE ** (jnp.arange(half, dtype=jnp.float32) / half))
    ang = positions.astype(jnp.float32)[..., None] * inv_freq
    cos, sin = jnp.cos(ang), jnp.sin(ang)
    q_pe = apply_rope(q_pe, cos[:, :, None, :], sin[:, :, None, :])
    k_pe = apply_rope(k_rope, cos, sin)[:, :, None, :]
    q_full = jnp.concatenate([q_nope, q_pe], axis=-1)
    k_full = jnp.concatenate(
        [k_nope, jnp.broadcast_to(k_pe, (b, s, MLA_HEADS, MLA_ROPE))], axis=-1)
    y_b = block_attention(q_full, k_full, v)

    return jnp.concatenate([y_a, y_b], axis=-1) @ w_out

def conformer_conv(h, w_pw1, b_pw1, w_dw, b_dw, ln_g, ln_b, w_pw2, b_pw2):
    u = h @ w_pw1 + b_pw1
    a, g = jnp.split(u, 2, axis=-1)
    u = a * jax.nn.sigmoid(g)
    u = depthwise_conv(u, w_dw) + b_dw
    u = jax.nn.silu(layer_norm(u, ln_g, ln_b))
    return u @ w_pw2 + b_pw2

def squared_relu_mlp(h, w1, w2):
    return jnp.square(jax.nn.relu(h @ w1)) @ w2

def first_inputs(seed: int = 0) -> dict:
    key = jax.random.key(seed)
    ks = jax.random.split(key, 24)

    def nrm(k, shape, fan_in):
        return jax.random.normal(k, shape, jnp.float32) * (fan_in ** -0.5)

    def gain(k, shape):
        return 1.0 + 0.05 * jax.random.normal(k, shape, jnp.float32)

    def bias(k, shape):
        return 0.02 * jax.random.normal(k, shape, jnp.float32)

    x = jax.random.normal(ks[0], (BATCH, SEQ, D_MODEL), jnp.float32)
    offsets = jax.random.randint(ks[1], (BATCH, 1), 0, SEQ, dtype=jnp.int32)
    positions = jnp.arange(SEQ, dtype=jnp.int32)[None, :] + offsets
    return {
        "x": x,
        "positions": positions,
        "sandwich_gains": gain(ks[2], (DEPTH, 4, D_MODEL)),
        "even_w_in": nrm(ks[3], (N_EVEN, D_MODEL, IN_COLS), D_MODEL),
        "even_sc_kernel": nrm(ks[4], (N_EVEN, SC_KERNEL, SC_WIDTH), SC_KERNEL),
        "even_q_norm": gain(ks[5], (N_EVEN, MLA_Q_RANK)),
        "even_w_uq": nrm(ks[6], (N_EVEN, MLA_Q_RANK, MLA_HEADS * (MLA_NOPE + MLA_ROPE)), MLA_Q_RANK),
        "even_kv_norm": gain(ks[7], (N_EVEN, MLA_KV_RANK)),
        "even_w_ukv": nrm(ks[8], (N_EVEN, MLA_KV_RANK, MLA_HEADS * (MLA_NOPE + MLA_V)), MLA_KV_RANK),
        "even_w_out": nrm(ks[9], (N_EVEN, MIX_WIDTH, D_MODEL), MIX_WIDTH),
        "odd_w_pw1": nrm(ks[10], (N_ODD, D_MODEL, 2 * CONF_WIDTH), D_MODEL),
        "odd_b_pw1": bias(ks[11], (N_ODD, 2 * CONF_WIDTH)),
        "odd_w_dw": nrm(ks[12], (N_ODD, CONF_KERNEL, CONF_WIDTH), CONF_KERNEL),
        "odd_b_dw": bias(ks[13], (N_ODD, CONF_WIDTH)),
        "odd_ln_g": gain(ks[14], (N_ODD, CONF_WIDTH)),
        "odd_ln_b": bias(ks[15], (N_ODD, CONF_WIDTH)),
        "odd_w_pw2": nrm(ks[16], (N_ODD, CONF_WIDTH, D_MODEL), CONF_WIDTH),
        "odd_b_pw2": bias(ks[17], (N_ODD, D_MODEL)),
        "mlp_w1": nrm(ks[18], (DEPTH, D_MODEL, D_FF), D_MODEL),
        "mlp_w2": nrm(ks[19], (DEPTH, D_FF, D_MODEL), D_FF),
    }

def first_block(x, positions, sandwich_gains, even_w_in, even_sc_kernel, even_q_norm,
              even_w_uq, even_kv_norm, even_w_ukv, even_w_out, odd_w_pw1, odd_b_pw1,
              odd_w_dw, odd_b_dw, odd_ln_g, odd_ln_b, odd_w_pw2, odd_b_pw2,
              mlp_w1, mlp_w2):
    for i in range(DEPTH):
        g = sandwich_gains[i]
        j = i // 2
        h = rms_norm(x, g[0])
        if i % 2 == 0:
            m = parallel_conv_mla(h, positions, even_w_in[j], even_sc_kernel[j],
                                  even_q_norm[j], even_w_uq[j], even_kv_norm[j],
                                  even_w_ukv[j], even_w_out[j])
        else:
            m = conformer_conv(h, odd_w_pw1[j], odd_b_pw1[j], odd_w_dw[j], odd_b_dw[j],
                               odd_ln_g[j], odd_ln_b[j], odd_w_pw2[j], odd_b_pw2[j])
        x = x + rms_norm(m, g[1])
        h = rms_norm(x, g[2])
        x = x + rms_norm(squared_relu_mlp(h, mlp_w1[i], mlp_w2[i]), g[3])
    return x


DEPTH_2 = 1

CHUNK = 64
N_META = 16
D_MIX = D_MODEL
D_ATTN = D_MIX // 2
HEAD_DIM = 64
N_HEADS = D_ATTN // HEAD_DIM
D_POOL = D_MIX - D_ATTN
POOL_WINDOWS = (2, 4, 8, 16)
N_POOL_GROUPS = len(POOL_WINDOWS)
POOL_GROUP_DIM = D_POOL // N_POOL_GROUPS
D_IN = 3 * D_ATTN + N_HEADS + D_POOL
D_FF_2 = ((8 * D_MODEL + 3 * 256 - 1) // (3 * 256)) * 256


def _rmsnorm(x, w):
    x32 = x.astype(jnp.float32)
    y = x32 * lax.rsqrt(jnp.mean(x32 * x32, axis=-1, keepdims=True) + EPS)
    return (y * w.astype(jnp.float32)).astype(x.dtype)

def _forgetting_attention(q, k, v, cum_logf):
    L = q.shape[2]
    scale = HEAD_DIM ** -0.5
    outs = []
    for q0 in range(0, L, Q_BLOCK):
        q1 = min(q0 + Q_BLOCK, L)
        qb = q[:, :, q0:q1]
        kp = k[:, :, :q1]
        vp = v[:, :, :q1]
        s = jnp.einsum("bhqd,bhkd->bhqk", qb, kp).astype(jnp.float32) * scale
        s = s + (cum_logf[:, :, q0:q1, None] - cum_logf[:, :, None, :q1])
        t_idx = jnp.arange(q0, q1)[:, None]
        s_idx = jnp.arange(q1)[None, :]
        s = jnp.where(s_idx <= t_idx, s, -jnp.inf)
        p = jax.nn.softmax(s, axis=-1).astype(v.dtype)
        outs.append(jnp.einsum("bhqk,bhkd->bhqd", p, vp))
    return jnp.concatenate(outs, axis=2)

def _trailing_mean_minus_self(u, window):
    L = u.shape[1]
    cs = jnp.concatenate([jnp.zeros_like(u[:, :1]), jnp.cumsum(u, axis=1)], axis=1)
    t = jnp.arange(L)
    lo = jnp.maximum(t + 1 - window, 0)
    total = cs[:, 1:] - cs[:, lo]
    count = (t + 1 - lo).astype(jnp.float32)[None, :, None]
    return total / count - u

def _layer(h, norm1_w, w_in, b_fgate, q_norm_w, k_norm_w, w_pool, pool_scale,
           w_out, norm2_w, w_gate, w_up, w_down):
    B, L, _ = h.shape
    n1 = _rmsnorm(h, norm1_w)
    proj = n1 @ w_in.astype(h.dtype)
    q, k, v, fg, u = jnp.split(
        proj, [D_ATTN, 2 * D_ATTN, 3 * D_ATTN, 3 * D_ATTN + N_HEADS], axis=-1)

    q = _rmsnorm(q.reshape(B, L, N_HEADS, HEAD_DIM), q_norm_w).transpose(0, 2, 1, 3)
    k = _rmsnorm(k.reshape(B, L, N_HEADS, HEAD_DIM), k_norm_w).transpose(0, 2, 1, 3)
    v = v.reshape(B, L, N_HEADS, HEAD_DIM).transpose(0, 2, 1, 3)
    log_f = jax.nn.log_sigmoid((fg + b_fgate.astype(fg.dtype)).astype(jnp.float32))
    cum_logf = jnp.cumsum(log_f.transpose(0, 2, 1), axis=-1)
    a_out = _forgetting_attention(q, k, v, cum_logf)
    a_out = a_out.transpose(0, 2, 1, 3).reshape(B, L, D_ATTN)

    u32 = u.astype(jnp.float32)
    pooled = jnp.stack(
        [_trailing_mean_minus_self(u32[..., g * POOL_GROUP_DIM:(g + 1) * POOL_GROUP_DIM], w)
         for g, w in enumerate(POOL_WINDOWS)], axis=2).astype(h.dtype)
    p_out = jnp.einsum("blgc,gcd->blgd", pooled, w_pool.astype(h.dtype)).reshape(B, L, D_POOL)
    p_out = p_out * pool_scale.astype(h.dtype)

    mix = jnp.concatenate([a_out, p_out], axis=-1) @ w_out.astype(h.dtype)
    h = h + mix

    n2 = _rmsnorm(h, norm2_w)
    ffn = (jax.nn.silu(n2 @ w_gate.astype(h.dtype)) * (n2 @ w_up.astype(h.dtype))) @ w_down.astype(h.dtype)
    return h + ffn

def second_inputs(seed: int = 0) -> dict:
    key = jax.random.key(seed)
    ks = jax.random.split(key, 16)
    x = jax.random.normal(ks[0], (BATCH, SEQ, D_MODEL), jnp.float32)
    meta_tokens = jax.random.normal(ks[1], (N_META, D_MODEL), jnp.float32)
    norm1_w = 1.0 + 0.05 * jax.random.normal(ks[2], (DEPTH_2, D_MODEL), jnp.float32)
    w_in = jax.random.normal(ks[3], (DEPTH_2, D_MODEL, D_IN), jnp.float32) * D_MODEL ** -0.5
    w_in = w_in.at[:, :, 3 * D_ATTN:3 * D_ATTN + N_HEADS].multiply(0.1)
    b_fgate = 2.0 + 2.0 * jax.random.uniform(ks[4], (DEPTH_2, N_HEADS), jnp.float32)
    q_norm_w = 1.0 + 0.05 * jax.random.normal(ks[5], (DEPTH_2, HEAD_DIM), jnp.float32)
    k_norm_w = 1.0 + 0.05 * jax.random.normal(ks[6], (DEPTH_2, HEAD_DIM), jnp.float32)
    w_pool = jax.random.normal(ks[7], (DEPTH_2, N_POOL_GROUPS, POOL_GROUP_DIM, POOL_GROUP_DIM),
                               jnp.float32) * POOL_GROUP_DIM ** -0.5
    pool_scale = 1.0 + 0.1 * jax.random.normal(ks[8], (DEPTH_2, D_POOL), jnp.float32)
    w_out = jax.random.normal(ks[9], (DEPTH_2, D_MIX, D_MODEL), jnp.float32) * D_MIX ** -0.5
    norm2_w = 1.0 + 0.05 * jax.random.normal(ks[10], (DEPTH_2, D_MODEL), jnp.float32)
    w_gate = jax.random.normal(ks[11], (DEPTH_2, D_MODEL, D_FF_2), jnp.float32) * D_MODEL ** -0.5
    w_up = jax.random.normal(ks[12], (DEPTH_2, D_MODEL, D_FF_2), jnp.float32) * D_MODEL ** -0.5
    w_down = jax.random.normal(ks[13], (DEPTH_2, D_FF_2, D_MODEL), jnp.float32) * D_FF_2 ** -0.5
    return {"x": x, "meta_tokens": meta_tokens, "norm1_w": norm1_w, "w_in": w_in,
            "b_fgate": b_fgate, "q_norm_w": q_norm_w, "k_norm_w": k_norm_w,
            "w_pool": w_pool, "pool_scale": pool_scale, "w_out": w_out,
            "norm2_w": norm2_w, "w_gate": w_gate, "w_up": w_up, "w_down": w_down}

def second_block(x, meta_tokens, norm1_w, w_in, b_fgate, q_norm_w, k_norm_w, w_pool,
              pool_scale, w_out, norm2_w, w_gate, w_up, w_down):
    B = x.shape[0]
    meta = jnp.broadcast_to(meta_tokens.astype(x.dtype)[None], (B, N_META, D_MODEL))
    h = jnp.concatenate([meta, x], axis=1)
    for layer in range(DEPTH_2):
        h = _layer(h, norm1_w[layer], w_in[layer], b_fgate[layer], q_norm_w[layer],
                   k_norm_w[layer], w_pool[layer], pool_scale[layer], w_out[layer],
                   norm2_w[layer], w_gate[layer], w_up[layer], w_down[layer])
    return h[:, N_META:]


def setup_inputs(seed=0):
    out = dict(first_inputs(seed))
    for name, value in second_inputs(seed + 1).items():
        if name != "x":
            out[name + "_2"] = value
    return out


def reference(
    x, positions, sandwich_gains, even_w_in, even_sc_kernel, even_q_norm, even_w_uq,
    even_kv_norm, even_w_ukv, even_w_out, odd_w_pw1, odd_b_pw1, odd_w_dw, odd_b_dw, odd_ln_g,
    odd_ln_b, odd_w_pw2, odd_b_pw2, mlp_w1, mlp_w2, meta_tokens_2, norm1_w_2, w_in_2, b_fgate_2,
    q_norm_w_2, k_norm_w_2, w_pool_2, pool_scale_2, w_out_2, norm2_w_2, w_gate_2, w_up_2,
    w_down_2,
):
    x = first_block(
        x, positions, sandwich_gains, even_w_in, even_sc_kernel, even_q_norm, even_w_uq,
        even_kv_norm, even_w_ukv, even_w_out, odd_w_pw1, odd_b_pw1, odd_w_dw, odd_b_dw,
        odd_ln_g, odd_ln_b, odd_w_pw2, odd_b_pw2, mlp_w1, mlp_w2,
    )
    return second_block(
        x, meta_tokens_2, norm1_w_2, w_in_2, b_fgate_2, q_norm_w_2, k_norm_w_2, w_pool_2,
        pool_scale_2, w_out_2, norm2_w_2, w_gate_2, w_up_2, w_down_2,
    )


_drawn_inputs = setup_inputs


def setup_inputs(seed=0):
    import zlib

    import numpy as np

    out = dict(_drawn_inputs(seed))
    spreads = {}
    factors = {'even_q_norm': 8.0,
     'even_kv_norm': 8.0,
     'odd_b_pw1': 4.906,
     'odd_b_dw': 2.672,
     'odd_ln_b': 5.287,
     'odd_b_pw2': 3.254,
     'meta_tokens_2': 3.384,
     'norm1_w_2': 3.858,
     'q_norm_w_2': 8.0,
     'k_norm_w_2': 8.0,
     'norm2_w_2': 3.206}
    for name, (base, spread) in spreads.items():
        noise = np.random.default_rng([zlib.crc32(name.encode()), seed]).standard_normal(out[name].shape)
        drawn = base * np.exp(spread * noise) if base else spread * noise
        out[name] = __import__('jax').numpy.asarray(drawn.astype(out[name].dtype))
    for name, factor in factors.items():
        out[name] = (out[name] * factor).astype(out[name].dtype)
    return out
```

```python
from contextlib import ExitStack

import numpy as np

import concourse.bass as bass
from concourse import mybir

F32 = mybir.dt.float32
F32R = mybir.dt.float32r
I32 = mybir.dt.int32
ALU = mybir.AluOpType
ACT = mybir.ActivationFunctionType
AX = mybir.AxisListType

P = 128
D = 1024
S = 512
KT = D // P
EPS = 1e-6
NEG = -1e30
RING = 4
SLOTS = 8

SCW = 512
QR, KVR, ROPE, HEADS, NOPE, DV = 384, 256, 32, 8, 64, 64
QK = NOPE + ROPE
HALF = ROPE // 2
K_ROPE_DMAS, Q_ROPE_DMAS = 2 * 2 * 2, 2 * 2 * HEADS
TAPS = 31
PAD = TAPS // 2
PE_TAPS = 8
DVE_TAPS = 18
POOL_TAPS = TAPS - PE_TAPS - DVE_TAPS
FF = 4096
CHUNK = 16
NCHUNK = FF // P // CHUNK
META = 16
HD = 64
WINDOWS = (2, 4, 8, 16)
L2 = META + S
DECAY_DMAS = HEADS * 2 * 2
FF2 = 2816
HT2 = FF2 // P

_COLS = [("gains", 64), ("norm1_2", 8), ("norm2_2", 8), ("b_pw1", 16), ("w_dw", 8 * TAPS), ("b_dw", 8),
         ("ln_g", 8), ("ln_b", 8), ("b_pw2", 8), ("sc", 12), ("q_norm", 3), ("kv_norm", 2),
         ("pool_scale", 4), ("q_norm_2", 1), ("k_norm_2", 1), ("b_fgate", 1), ("inv_freq", 1)]
COL, NCOL = {}, 0
for _name, _n in _COLS:
    COL[_name] = NCOL
    NCOL += _n

_PHASES = [("w_in", 19, 19), ("up_q", 3, 6), ("up_kn", 1, 4), ("up_v", 1, 4), ("w_out", 8, 8)]
for _c in range(NCHUNK):
    _PHASES += [(f"mlp0_up{_c}", CHUNK, CHUNK), (f"mlp0_down{_c}", 8 * CHUNK // SLOTS, 8)]
_PHASES += [("pw1", 16 + KT, 16 + KT), ("pw2", 8, 8)]
for _c in range(NCHUNK):
    _PHASES += [(f"mlp1_up{_c}", CHUNK, CHUNK), (f"mlp1_down{_c}", 8 * CHUNK // SLOTS, 8)]
_PHASES += [("w_in_2", 10, 10), ("pool", 1, 4), ("w_in_2b", 7, 7), ("w_out_2", 8, 8), ("ffn_up", 2 * HT2, 2 * HT2), ("ffn_down", 24, 8)]
BLOCK0, TILE0 = {}, {}
NBLK = NTILE = 0
for _name, _b, _t in _PHASES:
    BLOCK0[_name], TILE0[_name] = NBLK, NTILE
    NBLK += _b
    NTILE += _t

_JOBS = [("x0", KT, D), ("q_lat", 3, QR), ("kv_lat", 2, KVR), ("meta", 1, D), ("m1", KT, D), ("x1", KT, D),
         ("m2", KT, D), ("x2", KT, D), ("ln", KT, D), ("m3", KT, D), ("x3", KT, D), ("m4", KT, D),
         ("x4", KT, D), ("x5", KT, D)]
JOB = {name: i for i, (name, _, _) in enumerate(_JOBS)}
SSQ_ADDS = [sum(t - (name[0] == "x") for name, t, _ in _JOBS[:i + 1]) for i in range(len(_JOBS))]
JOB_D = [d for _, _, d in _JOBS]
OPERANDS = ["x0", "x1", "x2", "ln", "x3", "x4", "x5"]
OPN = {name: i for i, name in enumerate(OPERANDS)}
ENTRIES = ["x0", "x1", "x2", "x3", "x4", "x5"]
R2N = {name: i for i, name in enumerate(ENTRIES)}

PW1 = [("a", 0), ("g", 0), ("a", 1), ("g", 1), ("c", 0)]
for _j in range(2, KT):
    PW1 += [("a", _j), ("g", _j), ("c", _j - 1)]
PW1 += [("c", KT - 1)]
SQUARES = {name: KT * i for i, name in enumerate(OPERANDS)}
PW1_BLOCK, PW1_TILE = {}, {}
_b = 0
for _i, _x in enumerate(PW1):
    PW1_TILE[_x] = _i
    PW1_BLOCK[_x] = _b
    _b += 1

W_IN_2A = [("q", i) for i in range(4)] + [("f", 0)] + [("u", i) for i in range(4)] + [("k", 0)]
W_IN_2B = [("k", i) for i in range(1, 4)] + [("v", i) for i in range(4)]
HEAD_TILE = [TILE0["w_in_2"] + i for i in (0, 1, 2, 3, 9)] + [TILE0["w_in_2b"] + i for i in range(3)]
W_STAT, W_FACTOR, W_UPDATE, W_MEAN, W_CENTRE, W_VALUES = 10, 3, 16, 24, 48, (4, 4)
P_OUT_STEPS = 4


def build(nc, x_t, meta_t, positions, vectors, weights, out_t):
    ctx = ExitStack()
    with ctx:
        def sb(name, shape, dt=F32):
            return ctx.enter_context(nc.sbuf_tensor(name, shape, dt))

        def sem(name):
            return ctx.enter_context(nc.semaphore(name))

        KB = 1024
        arena = sb("arena", [P, 88 * KB // 4])
        raw = sb("raw", [P, RING, SLOTS, P])
        wh = sb("wh", [P, RING, SLOTS, P], F32R)
        wl = sb("wl", [P, RING, SLOTS, P], F32R)
        X = sb("X", [P, KT, S])
        m_area = sb("m_area", [P, 16 * KB // 4])
        XH = sb("XH", [P, KT, S], F32R)
        XL = sb("XL", [P, KT, S], F32R)
        tmp = sb("tmp", [P, 2, S])
        sqb = sb("sqb", [P, 2, S])
        ssq = sb("ssq", [P, S])
        hexp = sb("hexp", [P, 4, P])
        r2 = sb("r2", [P, S])
        ident = sb("ident", [P, P])
        ones = sb("ones", [P, P])
        headones = sb("headones", [P, P])
        ident_r = sb("ident_r", [P, P], F32R)
        mask_r = sb("mask_r", [P, P], F32R)
        vec = sb("vec", [P, NCOL])
        meta = sb("meta", [P, KT, META])
        meta_h = sb("meta_h", [P, KT, META], F32R)
        meta_l = sb("meta_l", [P, KT, META], F32R)
        meta_n = sb("meta_n", [P, KT, META])
        sd = sb("sd", [P, 4])
        rcol = sb("rcol", [P, len(_JOBS), 4])
        meta_x = sb("meta_x", [META, P])
        hcol = sb("hcol", [P, 2, 10])
        cols = sb("cols", [P, 4, 3])


        def at(name, base, off, shape, dt=F32):
            return nc.alloc_sbuf_tensor_at(name, shape, dt, offset=base + off)

        A = nc.lookup_mloc(arena).addr
        MA = nc.lookup_mloc(m_area).addr
        QH = at("QH", A, 0, [P, HEADS, S], F32R)
        QL = at("QL", A, 16 * KB, [P, HEADS, S], F32R)
        KH = at("KH", A, 32 * KB, [P, HEADS, S], F32R)
        KL = at("KL", A, 48 * KB, [P, HEADS, S], F32R)
        VH = at("VH", A, 64 * KB, [P, 4, S], F32R)
        VL = at("VL", A, 72 * KB, [P, 4, S], F32R)
        PH = at("PH", A, 80 * KB, [P, 2, 4, 2 * P], F32R)
        lat = at("lat", A, 0, [P, 5, S])
        gate_c = at("gate_c", A, 10 * KB, [P, 4, S])
        gated = at("gated", A, 18 * KB, [P, 4, S + 2])
        LH = at("LH", A, 64 * KB, [P, 5, S], F32R)
        LL = at("LL", A, 74 * KB, [P, 5, S], F32R)
        trig = at("trig", A, 84 * KB, [P, 2, S])
        y_conv = at("y_conv", MA, 0, [P, 4, S])
        rope_h = at("rope_h", MA, 8 * KB, [P, 2, S], F32R)
        rope_l = at("rope_l", MA, 12 * KB, [P, 2, S], F32R)
        prob = at("prob", MA, 0, [P, 4, S])
        PL = at("PL", MA, 8 * KB, [P, 2, 4, 2 * P], F32R)
        M = at("M", MA, 0, [P, KT, S])
        pos_i = at("pos_i", MA, 0, [P, S], I32)
        ang = at("ang", MA, 2 * KB, [P, S])
        turns = at("turns", MA, 4 * KB, [P, S])
        HH = at("HH", A, 0, [P, HT2, S], F32R)
        HL = at("HL", A, 44 * KB, [P, HT2, S], F32R)
        UW = S + 2 * PAD
        U = at("U", A, 0, [P, 2, UW])
        UH = at("UH", A, 6 * KB, [P, 2, UW], F32R)
        UL = at("UL", A, 12 * KB, [P, 2, UW], F32R)
        conv = at("conv", A, 18 * KB, [P, KT, S])
        acc = at("acc", A, 34 * KB, [P, 2, 2, S])
        sum1 = at("sum1", A, 42 * KB, [P, S])
        acc_p = at("acc_p", A, 44 * KB, [P, 2, S])
        tapped = at("tapped", A, 48 * KB, [P, POOL_TAPS - 1, S])
        Q2H = at("Q2H", A, 0, [P, 4, S], F32R)
        Q2L = at("Q2L", A, 8 * KB, [P, 4, S], F32R)
        K2H = at("K2H", A, 16 * KB, [P, 4, L2], F32R)
        K2L = at("K2L", A, 25 * KB, [P, 4, L2], F32R)
        V2H = at("V2H", A, 34 * KB, [P, 5, S], F32R)
        V2L = at("V2L", A, 44 * KB, [P, 5, S], F32R)
        P2H = at("P2H", A, 54 * KB, [P, 2, 5, 2 * P], F32R)
        P2L = at("P2L", A, 64 * KB, [P, 2, 5, 2 * P], F32R)
        CQ = at("CQ", A, 74 * KB, [P, 2, S], F32R)
        CK = at("CK", A, 78 * KB, [P, 2, L2], F32R)
        cum_h = at("cum_h", A, 83 * KB, [HEADS, L2], F32R)
        cum_l = at("cum_l", A, 85 * KB + 512, [HEADS, L2], F32R)
        pooled = at("pooled", A, 54 * KB, [P, 4, S])
        logf = at("logf", A, 62 * KB, [HEADS, 3, L2])
        u2 = at("u2", A, 69 * KB, [P, L2])
        head_t = at("head_t", MA, 0, [P, 4, L2])
        head_q = at("head_q", MA, 8 * KB + 512, [P, L2])
        pool_a = at("pool_a", MA, 11 * KB, [P, 2, L2])
        pool_h = at("pool_h", A, 34 * KB, [P, 4, S], F32R)
        pool_l = at("pool_l", A, 44 * KB, [P, 4, S], F32R)
        prob2 = at("prob2", MA, 0, [P, 3, L2])

        PS = ctx.enter_context(nc.psum_tensor("PS", [P, 8, S], F32))
        STAT, RB, HB, META_BANK = 4, 5, 6, 7

        def gain(layer, which, k):
            return vec[:, COL["gains"] + (layer * 4 + which) * KT + k:][:, 0:1]

        def col(name, i=0):
            return vec[:, COL[name] + i:COL[name] + i + 1]

        ENTRY_GAIN = {"x0": lambda k: gain(0, 0, k), "x1": lambda k: gain(0, 2, k), "x2": lambda k: gain(1, 0, k),
                      "x3": lambda k: gain(1, 2, k), "x4": lambda k: col("norm1_2", k), "x5": lambda k: col("norm2_2", k)}
        M_GAIN = {"x1": lambda k: gain(0, 1, k), "x2": lambda k: gain(0, 3, k), "x3": lambda k: gain(1, 1, k),
                  "x4": lambda k: gain(1, 3, k)}

        def p_out(t):
            return (tmp, sqb)[t // 2][:, t % 2]

        vec_in, meta_in, pos_in = sem("vec_in"), sem("meta_in"), sem("pos_in")
        x_in = [sem(f"x_in{k}") for k in range(KT)]
        raw_in = [sem(f"raw_in{j}") for j in range(RING)]
        consts = sem("consts")
        consts_r = sem("consts_r")
        w_hi = sem("w_hi")
        w_lo = sem("w_lo")
        blocks_done = sem("blocks_done")
        bank_free = sem("bank_free")
        x_new = sem("x_new")
        xh = sem("xh")
        xl = sem("xl")
        squares = sem("squares")
        ssq_adds = sem("ssq_adds")
        stat_done = sem("stat_done")
        sd_done = sem("sd_done")
        rcol_done = sem("rcol_done")
        rb_done = sem("rb_done")
        r2_done = sem("r2_done")
        dve = sem("dve")
        act = sem("act")
        angles = sem("angles")
        trig_done = sem("trig_done")
        meta_split = sem("meta_split")
        lat_done = sem("lat_done")
        rope_done = sem("rope_done")
        y_ready = sem("y_ready")
        rows_zero = sem("rows_zero")
        kpe_in, qpe_in = sem("kpe_in"), sem("qpe_in")
        ev_hi = sem("ev_hi")
        ev_lo = sem("ev_lo")
        s_done, neg_max, exp_done = sem("s_done"), sem("neg_max"), sem("exp_done")
        inv_sum, p_done = sem("inv_sum"), sem("p_done")
        t_done, ph_done, pl_done, pv_done = sem("t_done"), sem("ph_done"), sem("pl_done"), sem("pv_done")
        yh_done, yl_done = sem("yh_done"), sem("yl_done")
        hid = sem("hid")
        gate_z, gate_s = sem("gate_z"), sem("gate_s")
        u_done, uh_done, ul_done = sem("u_done"), sem("uh_done"), sem("ul_done")
        products_done = sem("products_done")
        pool_taps, dve_taps = sem("pool_taps"), sem("dve_taps")
        taps_done = sem("taps_done")
        conv_done = sem("conv_done")
        sum1_done, mean_done, centred = sem("sum1_done"), sem("mean_done"), sem("centred")
        ln_z, ln_s = sem("ln_z"), sem("ln_s")
        hsq, hstat, hsd, hexp_done, hb_done = sem("hsq"), sem("hstat"), sem("hsd"), sem("hexp_done"), sem("hb_done")
        heads_done = sem("heads_done")
        v_meta_free = sem("v_meta_free")
        p_out_h, p_out_l = sem("p_out_h"), sem("p_out_l")
        fz, fexp, cum_done, decay_in = sem("fz"), sem("fexp"), sem("cum_done"), sem("decay_in")
        pooled_done, pool_hi, pool_lo = sem("pooled_done"), sem("pool_hi"), sem("pool_lo")
        out_done = sem("out_done")

        block = ctx.enter_context(nc.Block())
        UNITS = HEADS * 4

        def score_area(layer, u):
            if layer == 0:
                return PS[:, (0, 1, 5)[u % 3]]
            if u % 4 < 3:
                return PS[:, 2 * (u % 2), 0:P * (u % 4 + 1) + META]
            return PS[:, 2:4].rearrange("p b n -> p (b n)")[:, S - 3 * P - META:S + P]

        def turned_area(layer, u):
            if layer == 0:
                return PS[:, (2, 3, 4)[u % 3]].rearrange("p (k q) -> p k q", q=P), None
            i = u % 4
            return (PS[:, (4, 1)[u % 2], 0:P * (i + 1)].rearrange("p (k q) -> p k q", q=P),
                    PS[0:META, (5, 7)[u % 2], 0:P])

        def result_bank(layer, h):
            return 6 + h % 2 if layer == 0 else 6

        @block.sync
        def _(sp):
            sp.dma_start(vec[:], vectors).then_inc(vec_in, 16)
            for n in range(2):
                sp.dma_start(raw[:, n], weights[n]).then_inc(raw_in[n], 16)
            for k in range(KT):
                sp.dma_start(X[:, k], x_t[:, k]).then_inc(x_in[k], 16)
                if k == 0:
                    sp.dma_start(raw[:, 2], weights[2]).then_inc(raw_in[2], 16)
            sp.dma_start(raw[:, 3], weights[3]).then_inc(raw_in[3], 16)
            sp.dma_start(pos_i[:], positions.broadcast_to((P, S))).then_inc(pos_in, 16)
            sp.dma_start(meta[:], meta_t).then_inc(meta_in, 16)

            def load(n):
                sp.wait_ge(w_lo, n - RING + 1)
                sp.dma_start(raw[:, n % RING], weights[n]).then_inc(raw_in[n % RING], 16)

            def load_range(a, b):
                while a % RING:
                    load(a)
                    a += 1
                with sp.Fori(a // RING, b // RING, 1) as g:
                    for j in range(RING):
                        sp.wait_ge(w_lo, g * RING + (j - RING + 1))
                        sp.dma_start(raw[:, j], weights[g * RING + j]).then_inc(raw_in[j], 16)
                for n in range(b // RING * RING, b):
                    load(n)

            load_range(RING, 16)
            sp.wait_ge(rope_done, 1)
            for src, dst in ((rope_h, KH), (rope_l, KL)):
                by_parity = dst[:].bitcast(F32).rearrange("p (h two) s -> p two h s", two=2)
                for half in range(2):
                    for odd in range(2):
                        row = (0 if odd else NOPE) + half * HALF
                        sp.dma_start(by_parity[row:row + HALF, odd],
                                     src[0:HALF, half].bitcast(F32).unsqueeze(1).broadcast_to((HALF, HEADS // 2, S))
                                     ).then_inc(kpe_in, 16)
            load_range(16, BLOCK0["w_out"] + 4)
            sp.wait_ge(rope_done, 2)
            for src, dst in ((rope_h, QH), (rope_l, QL)):
                for half in range(2):
                    for h in range(HEADS):
                        row = (0 if h % 2 else NOPE) + half * HALF
                        sp.dma_start(dst[row:row + HALF, h].bitcast(F32),
                                     src[h * HALF:(h + 1) * HALF, half].bitcast(F32)).then_inc(qpe_in, 16)
            load_range(BLOCK0["w_out"] + 4, BLOCK0["w_in_2"] + 14)
            sp.wait_ge(cum_done, 1)
            for b in range(2):
                for r, cum in ((0, cum_h), (1, cum_l)):
                    for a in range(4):
                        row = cum[4 * b + a:4 * b + a + 1].bitcast(F32)
                        q0, k0 = 32 * a + r, 32 * a + 2 + r
                        sp.dma_start(CQ[q0:q0 + 1, b].bitcast(F32), row[:, META:L2]).then_inc(decay_in, 16)
                        sp.dma_start(CK[k0:k0 + 1, b].bitcast(F32), row).then_inc(decay_in, 16)
            load_range(BLOCK0["w_in_2"] + 14, NBLK)
            for m in range(KT):
                sp.wait_ge(bank_free, TILE0["ffn_down"] + m + 1)
                sp.dma_start(out_t[:, m], X[:, m]).then_inc(out_done, 16)
            sp.wait_ge(out_done, 16 * KT)

        @block.gpsimd
        def _(pool):
            pool.memset(ident[:], 0.0).then_inc(consts, 1)
            pool.memset(ones[:], 1.0).then_inc(consts, 1)
            pool.memset(headones[:], 0.0).then_inc(consts, 1)
            pool.memset(hexp[:, 0], 0.0).then_inc(consts, 1)
            pool.wait_ge(consts, 4)
            pool.affine_select(out=ident[:], in_=ident[:], compare_op=ALU.not_equal, fill=1.0, base=0,
                               pattern=[[-1, P]], channel_multiplier=1).then_inc(consts, 1)
            pool.affine_select(out=hexp[:, 0], in_=hexp[:, 0], compare_op=ALU.is_ge, fill=NEG, base=0,
                               pattern=[[-1, P]], channel_multiplier=1).then_inc(consts, 1)
            for half in range(2):
                rows = slice(half * HD, (half + 1) * HD)
                pool.wait_ge(consts, 6 + half)
                pool.memset(headones[rows, rows], 1.0).then_inc(consts, 1)
            def lo_range(a, b):
                def lo(n):
                    pool.wait_ge(w_hi, n + 1)
                    pool.tensor_tensor(wl[:, n % RING], raw[:, n % RING], wh[:, n % RING].bitcast(F32),
                                       ALU.subtract).then_inc(w_lo, 1)
                while a % RING:
                    lo(a)
                    a += 1
                if b // RING > a // RING:
                    with pool.Fori(a // RING, b // RING, 1) as g:
                        for j in range(RING):
                            pool.wait_ge(w_hi, g * RING + (j + 1))
                            pool.tensor_tensor(wl[:, j], raw[:, j], wh[:, j].bitcast(F32), ALU.subtract).then_inc(w_lo, 1)
                for n in range(max(a, b // RING * RING), b):
                    lo(n)

            def zero_rows(parts, blocks, before):
                pool.wait_ge(w_lo, blocks)
                for i, t in enumerate(parts):
                    pool.memset(t[:].bitcast(F32).rearrange("p (h two) s -> p two h s", two=2)[32:64, 1],
                                0.0).then_inc(rows_zero, 1)
                    pool.wait_ge(rows_zero, before + i + 1)

            def normalise(layer):
                U0 = layer * UNITS
                for u in range(UNITS):
                    if layer == 0:
                        p = prob[:, u % 4]
                    else:
                        p = prob2[:, u % 3, 0:128 * (u % 4 + 1) + META]
                    pool.wait_ge(inv_sum, U0 + u + 1)
                    pool.tensor_tensor(p, p, cols[:, u % 4, 2:3].broadcast_to(p.shape), ALU.mult).then_inc(p_done, 1)

            def add_squares(entry):
                before = SSQ_ADDS[JOB[entry]] - (KT - 1)
                for k in range(1, KT):
                    pool.wait_ge(squares, SQUARES[entry] + k + 1)
                    if before + k - 1:
                        pool.wait_ge(ssq_adds, before + k - 1)
                    pool.tensor_tensor(ssq[:], ssq[:], sqb[:, k % 2], ALU.add).then_inc(ssq_adds, 1)

            for n in range(3):
                pool.wait_ge(w_hi, n + 1)
                pool.tensor_tensor(wl[:, n], raw[:, n], wh[:, n].bitcast(F32), ALU.subtract).then_inc(w_lo, 1)
            add_squares("x0")
            lo_range(3, 5)
            zero_rows((KH, KL), 5, 0)
            lo_range(5, BLOCK0["up_q"] + 2)
            pool.wait_ge(y_ready, 4)
            zero_rows((QH, QL), BLOCK0["up_q"] + 2, 2)
            lo_range(BLOCK0["up_q"] + 2, BLOCK0["w_out"] + 4)
            normalise(0)
            n0 = BLOCK0["pw1"]
            lo_range(BLOCK0["w_out"] + 4, BLOCK0["mlp0_up0"] + 4)
            add_squares("x1")
            lo_range(BLOCK0["mlp0_up0"] + 4, n0 + 4)
            add_squares("x2")
            done = n0 + 4

            def lo_to(n):
                nonlocal done
                for i in range(done, n):
                    pool.wait_ge(w_hi, i + 1)
                    pool.tensor_tensor(wl[:, i % RING], raw[:, i % RING], wh[:, i % RING].bitcast(F32),
                                       ALU.subtract).then_inc(w_lo, 1)
                done = max(done, n)

            def add_taps(j, first, last):
                a = acc_p[:, j % 2]
                for i in range(first, last):
                    pool.wait_ge(products_done, j * POOL_TAPS + i + 1)
                    if i > 1:
                        pool.wait_ge(pool_taps, j * (POOL_TAPS - 1) + i - 1)
                    pool.tensor_tensor(a, a, tapped[:, i - 1], ALU.add).then_inc(pool_taps, 1)

            def add_sum(j):
                pool.wait_ge(conv_done, j + 1)
                if j:
                    pool.wait_ge(sum1_done, j)
                    pool.tensor_tensor(sum1[:], sum1[:], conv[:, j], ALU.add).then_inc(sum1_done, 1)
                else:
                    pool.tensor_copy(sum1[:], conv[:, 0]).then_inc(sum1_done, 1)

            for j in range(KT):
                n = n0 + PW1_BLOCK[("g", j)]
                lo_to(n + 4)
                b = j % 2
                pool.wait_ge(uh_done, j + 1)
                if j >= 2:
                    pool.wait_ge(blocks_done, n0 + PW1_BLOCK[("c", j - 2)] + 1)
                pool.tensor_tensor(UL[:, b], U[:, b], UH[:, b].bitcast(F32), ALU.subtract).then_inc(ul_done, 1)
                add_taps(j, 1, 3)
                lo_to(n + 5)
                add_taps(j, 3, POOL_TAPS)
                pool.wait_ge(dve_taps, j + 1)
                pool.wait_ge(pool_taps, (j + 1) * (POOL_TAPS - 1))
                pool.tensor_tensor(acc_p[:, b], acc_p[:, b], acc[:, b, 1], ALU.add).then_inc(taps_done, 1)
                if j:
                    lo_to(n + 6)
                    add_sum(j - 1)
            add_sum(KT - 1)
            lo_range(done, BLOCK0["mlp1_up0"] + 4)
            add_squares("x3")
            lo_range(BLOCK0["mlp1_up0"] + 4, BLOCK0["w_in_2"] + 4)
            add_squares("x4")
            lo_range(BLOCK0["w_in_2"] + 4, BLOCK0["w_out_2"] + 4)
            normalise(1)
            lo_range(BLOCK0["w_out_2"] + 4, BLOCK0["ffn_up"] + 4)
            add_squares("x5")
            lo_range(BLOCK0["ffn_up"] + 4, NBLK)
        NCONST = 8

        @block.scalar
        def _(sc):
            chain = [0]

            def step(ins):
                chain[0] += 1
                ins.then_inc(act, 1)
                sc.wait_ge(act, chain[0])

            def hi(n):
                if n >= NBLK:
                    return
                j = n % RING
                sc.wait_ge(raw_in[j], 16 * (n // RING + 1))
                if n >= RING:
                    sc.wait_ge(blocks_done, n - RING + 1)
                sc.activation(wh[:, j], raw[:, j], ACT.Copy).then_inc(w_hi, 1)

            def hi_range(a, b):
                while a < b and a % RING:
                    hi(a)
                    a += 1
                rounds = (b - a) // RING
                if rounds > 1:
                    g0 = a // RING
                    with sc.Fori(g0, g0 + rounds, 1) as g:
                        for j in range(RING):
                            sc.wait_ge(raw_in[j], g * 16 + 16)
                            sc.wait_ge(blocks_done, g * RING + (j - RING + 1))
                            sc.activation(wh[:, j], raw[:, j], ACT.Copy).then_inc(w_hi, 1)
                    a += rounds * RING
                while a < b:
                    hi(a)
                    a += 1

            def root(job):
                n = JOB[job]
                rows, w = (META, 1) if job == "meta" else (P, 4)
                scale = QK if job == "q_lat" else 1.0
                sc.wait_ge(stat_done, n + 1)
                sc.activation(sd[0:rows, 0:w], PS[0:rows, STAT, 0:w], ACT.Sqrt, bias=EPS * scale,
                              scale=scale / JOB_D[n]).then_inc(sd_done, 1)

            def keep_r2(entry):
                sc.wait_ge(rb_done, JOB[entry] + 1)
                sc.activation(r2[:], PS[:, RB], ACT.Copy).then_inc(r2_done, 1)

            def operand(entry):
                o = OPN[entry]
                for k in range(KT):
                    if entry == "x0":
                        sc.wait_ge(x_in[k], 16)
                    elif entry == "x5":
                        sc.wait_ge(bank_free, TILE0["w_out_2"] + k + 1)
                    else:
                        sc.wait_ge(x_new, KT * (R2N[entry] - 1) + k + 1)
                    sc.activation(XH[:, k], X[:, k], ACT.Copy, scale=ENTRY_GAIN[entry](k)).then_inc(xh, 1)
                    if k == 0:
                        if JOB[entry]:
                            sc.wait_ge(stat_done, JOB[entry])
                        sc.activation(ssq[:], X[:, 0], ACT.Square).then_inc(squares, 1)
                        continue
                    added = SSQ_ADDS[JOB[entry]] - (KT - 1) + max(k - 2, 0)
                    if added:
                        sc.wait_ge(ssq_adds, added)
                    sc.activation(sqb[:, k % 2], X[:, k], ACT.Square).then_inc(squares, 1)

            def enter(phase, entry):
                n0 = BLOCK0[phase]
                hi(n0 + 4)
                root(entry)
                hi(n0 + 5)
                keep_r2(entry)
                hi(n0 + 6)
                hi(n0 + 7)

            sc.wait_ge(consts, NCONST)
            sc.activation(ident_r[:], ident[:], ACT.Copy).then_inc(consts_r, 1)
            sc.activation(mask_r[:], hexp[:, 0], ACT.Copy).then_inc(consts_r, 1)
            sc.wait_ge(vec_in, 16)
            for n in range(3):
                hi(n)
            operand("x0")
            hi(3)
            enter("w_in", "x0")
            root("q_lat")
            hi(8)
            sc.wait_ge(angles, 2)
            sc.activation(trig[:], trig[:], ACT.Sin).then_inc(trig_done, 1)
            hi(9)
            hi(10)
            hi(11)
            root("kv_lat")
            hi(12)
            hi(13)
            hi(14)
            root("meta")
            hi_range(15, BLOCK0["up_q"] + 4)
            ev = [0]

            def ev_copy(dst, src, **kw):
                ev[0] += 1
                sc.activation(dst, src, ACT.Copy, **kw).then_inc(ev_hi, 1)

            def heads_hi(dst, phase, t, done):
                b = (TILE0[phase] + t + (2 if phase == "up_q" else 0)) % 4
                sc.wait_ge(blocks_done, done)
                ev_copy(dst[0:NOPE, 2 * t], PS[0:NOPE, b])
                ev_copy(dst[NOPE:P, 2 * t + 1], PS[NOPE:P, b])

            nq = BLOCK0["up_q"]
            sc.wait_ge(y_ready, 4)
            hi(nq + 4)
            heads_hi(QH, "up_q", 0, nq + 2)
            heads_hi(QH, "up_q", 1, nq + 2)
            hi(nq + 5)
            heads_hi(QH, "up_q", 2, nq + 3)
            heads_hi(QH, "up_q", 3, nq + 3)
            hi(nq + 6)
            for t in range(4):
                heads_hi(KH, "up_kn", t, BLOCK0["up_kn"] + 1)
            hi(nq + 7)
            for t in range(4):
                sc.wait_ge(blocks_done, BLOCK0["up_v"] + 1)
                ev_copy(VH[:, t], PS[:, (TILE0["up_v"] + t) % 4])
            hi(nq + 8)
            for t in range(4):
                ev_copy(XH[:, t], y_conv[:, t])

            def attention(layer):
                U0, H0 = layer * UNITS, layer * HEADS
                bufs = 4 if layer == 0 else 3
                for s in range(UNITS + 6):
                    if s < UNITS:
                        sc.wait_ge(neg_max, U0 + s + 1)
                        if s >= bufs:
                            sc.wait_ge(t_done, U0 + s - bufs + 1)
                        p = prob[:, s % 4] if layer == 0 else prob2[:, s % 3, 0:128 * (s % 4 + 1) + META]
                        sc.activation(p, score_area(layer, s), ACT.Exp, bias=cols[:, s % 4, 0:1],
                                      accum_out=cols[:, s % 4, 1:2]).then_inc(exp_done, 1)
                    u = s - 3
                    if 0 <= u < UNITS:
                        pair, q = u // 2, slice(P * (u % 2), P * (u % 2) + P)
                        if pair >= 2:
                            sc.wait_ge(pv_done, U0 // 2 + pair - 1)
                        sc.wait_ge(t_done, U0 + u + 1)
                        main, small = turned_area(layer, u)
                        if layer == 0:
                            if u == 0:
                                sc.wait_ge(ev_lo, 12)
                            sc.activation(PH[:, pair % 2, :, q], main, ACT.Copy).then_inc(ph_done, 1)
                        else:
                            i = u % 4
                            sc.activation(P2H[0:META, pair % 2, 4, q], small, ACT.Copy).then_inc(act, 1)
                            sc.activation(P2H[:, pair % 2, 0:i + 1, q], main, ACT.Copy).then_inc(ph_done, 1)
                            chain[0] += 1
                    if layer == 1 and s % P_OUT_STEPS == 1 and s // P_OUT_STEPS < 4:
                        t = s // P_OUT_STEPS
                        sc.activation(XH[:, 4 + t], p_out(t), ACT.Copy).then_inc(p_out_h, 1)
                    if s >= 8 and s % 4 == 0:
                        h = (s - 8) // 4
                        rows = slice(64 * (h % 2), 64 * (h % 2) + 64)
                        sc.wait_ge(pv_done, U0 // 2 + 2 * h + 2)
                        sc.activation(XH[rows, (4 if layer == 0 else 0) + h // 2], PS[rows, result_bank(layer, h)],
                                      ACT.Copy).then_inc(yh_done, 1)

            attention(0)
            nw = BLOCK0["w_out"]
            hi_range(nq + 9, nw + 8 + 4)

            def boundary(entry):
                if entry in M_GAIN:
                    root("m" + entry[1])
                operand(entry)

            def mlp(layer, entry):
                boundary(entry)
                enter(f"mlp{layer}_up0", entry)
                hi_range(BLOCK0[f"mlp{layer}_up0"] + 8, BLOCK0[f"mlp{layer}_up0"] + 64 + 4)

            mlp(0, "x1")
            boundary("x2")
            n0 = BLOCK0["pw1"]
            enter("pw1", "x2")
            done = n0 + 8
            for i, (kind, j) in enumerate(PW1):
                if kind == "g":
                    sc.wait_ge(gate_z, j + 1)
                    sc.activation(sqb[:, 0], tmp[:, 1], ACT.Sigmoid, bias=col("b_pw1", KT + j)).then_inc(gate_s, 1)
                    sc.wait_ge(u_done, j + 1)
                    if j >= 2:
                        sc.wait_ge(blocks_done, n0 + PW1_BLOCK[("c", j - 2)] + 1)
                    sc.activation(UH[:, j % 2], U[:, j % 2], ACT.Copy).then_inc(uh_done, 1)
                    for t in range(POOL_TAPS):
                        if t == 0:
                            if j >= 2:
                                sc.wait_ge(conv_done, j - 1)
                            dst = acc_p[:, j % 2]
                        else:
                            if j:
                                sc.wait_ge(pool_taps, (j - 1) * (POOL_TAPS - 1) + t)
                            dst = tapped[:, t - 1]
                        first = PE_TAPS + DVE_TAPS + t
                        sc.activation(dst, U[:, j % 2, first:first + S], ACT.Copy,
                                      scale=col("w_dw", j * TAPS + first)).then_inc(products_done, 1)
                upto = n0 + i + 4
                hi_range(done, max(done, upto))
                done = max(done, upto)
            hi_range(done, BLOCK0["pw2"] + 4)
            for k in range(KT):
                sc.wait_ge(centred, k + 1)
                if k >= 2:
                    sc.wait_ge(ssq_adds, SSQ_ADDS[JOB["x2"]] + k - 1)
                sc.activation(sqb[:, k % 2], conv[:, k], ACT.Square).then_inc(squares, 1)
            root("ln")
            for k in range(KT):
                sc.wait_ge(ln_z, k + 1)
                if k >= 2:
                    sc.wait_ge(xl, KT * OPN["ln"] + k - 1)
                sc.activation(sqb[:, k % 2], tmp[:, k % 2], ACT.Silu, bias=col("ln_b", k)).then_inc(ln_s, 1)
                sc.wait_ge(ln_s, k + 1)
                sc.activation(XH[:, k], sqb[:, k % 2], ACT.Copy).then_inc(xh, 1)
            hi_range(BLOCK0["pw2"] + 4, BLOCK0["pw2"] + 8 + 4)
            mlp(1, "x3")
            boundary("x4")
            n0 = BLOCK0["w_in_2"]
            enter("w_in_2", "x4")

            def head_square(e):
                keys = e >= 4
                w = L2 if keys else S
                sc.wait_ge(bank_free, HEAD_TILE[e] + 1)
                if e:
                    sc.wait_ge(hstat, e)
                sc.activation(head_q[:, 0:w], head_t[:, e % 4, 0:w], ACT.Square).then_inc(hsq, 1)

            def head_root(e):
                keys = e >= 4
                scale = 1.0 if keys else float(HD)
                sc.wait_ge(hstat, e + 1)
                sc.activation(hcol[:, 0, 0:8], PS[:, STAT, 0:8], ACT.Sqrt, bias=EPS * scale,
                              scale=scale / HD).then_inc(act if keys else hsd, 1)
                if keys:
                    chain[0] += 1
                    sc.activation(hcol[0:META, 0, 8:10], PS[0:META, STAT, 8:10], ACT.Sqrt, bias=EPS * scale,
                                  scale=scale / HD).then_inc(hsd, 1)

            def pool_operand(t):
                sc.wait_ge(pooled_done, t + 1)
                sc.activation(pool_h[:, t], pooled[:, t], ACT.Copy).then_inc(pool_hi, 1)

            head_square(0)
            head_root(0)
            head_square(1)
            head_root(1)
            hi(n0 + 8)
            head_square(2)
            head_root(2)
            hi(n0 + 9)
            sc.wait_ge(fz, 1)
            sc.activation(logf[:, 1], logf[:, 1], ACT.Exp, scale=-1.0).then_inc(act, 1)
            chain[0] += 1
            sc.wait_ge(act, chain[0])
            sc.activation(logf[:, 1], logf[:, 1], ACT.Ln, bias=1.0).then_inc(fexp, 1)
            head_square(3)
            head_root(3)
            hi(n0 + 10)
            pool_operand(0)
            hi(n0 + 11)
            pool_operand(1)
            hi(n0 + 12)
            pool_operand(2)
            pool_operand(3)
            hi(n0 + 13)
            head_square(4)
            hi(n0 + 14)
            head_root(4)
            hi(n0 + 15)
            for e in range(5, 8):
                head_square(e)
                head_root(e)
                if e < 7:
                    hi(n0 + 11 + e)
            hi(n0 + 18)
            hi(n0 + 19)
            hi(n0 + 20)
            for t in range(4):
                sc.wait_ge(blocks_done, n0 + 18)
                sc.wait_ge(rcol_done, JOB["x4"] + 1)
                ev_copy(V2H[:, t], PS[:, (TILE0["w_in_2b"] + 3 + t) % 4], scale=rcol[:, JOB["x4"], t:t + 1])
            ev_copy(V2H[0:META, 4], PS[0:META, META_BANK])
            hi(n0 + 21)
            attention(1)
            hi_range(n0 + 22, BLOCK0["ffn_up"] + 4)
            sc.wait_ge(blocks_done, BLOCK0["ffn_up"])
            operand("x5")
            n0 = BLOCK0["ffn_up"]
            hi(n0 + 4)
            root("x5")
            hi(n0 + 5)
            keep_r2("x5")
            hi(n0 + 6)

            def silu(pair):
                sc.wait_ge(gate_z, pair + (KT + 1))
                sc.activation(sqb[:, 0], tmp[:, 0], ACT.Silu).then_inc(gate_s, 1)

            silu(0)
            hi(n0 + 7)
            silu(1)
            with sc.Fori(1, HT2 // 2, 1) as g:
                for j in range(RING):
                    n = g * RING + (n0 + 4 + j)
                    slot = (n0 + j) % RING
                    sc.wait_ge(raw_in[slot], g * 16 + 16 * ((n0 + 4 + j) // RING + 1))
                    sc.wait_ge(blocks_done, n - RING + 1)
                    sc.activation(wh[:, slot], raw[:, slot], ACT.Copy).then_inc(w_hi, 1)
                    if j % 2:
                        silu(g * 2 + j // 2)
            hi_range(n0 + 4 + 2 * HT2, NBLK)

        @block.vector
        def _(v):
            chain = [0]

            def step(ins):
                chain[0] += 1
                ins.then_inc(dve, 1)
                v.wait_ge(dve, chain[0])

            def sig(ins, s, n):
                ins.then_inc(s, 1)
                v.wait_ge(s, n)

            def tt(out, a, b, op):
                return v.tensor_tensor(out, a, b, op)

            def ts(out, a, s1, op0, s2=None, op1=None):
                if op1 is None:
                    return v.tensor_scalar(out, a, s1, None, op0)
                return v.tensor_scalar(out, a, s1, s2, op0, op1)

            def stt(out, a, s, b, op0, op1):
                return v.scalar_tensor_tensor(out=out, in0=a, scalar=s, in1=b, op0=op0, op1=op1)

            def f(ap):
                return ap.bitcast(F32)

            ssq_n = [0]

            def add_squares(src):
                ssq_n[0] += 1
                sig(tt(ssq[:], ssq[:], src, ALU.add), ssq_adds, ssq_n[0])

            def clear_ssq(job):
                if JOB[job]:
                    v.wait_ge(stat_done, JOB[job])
                step(v.memset(ssq[:], 0.0))

            def factor(job):
                n = JOB[job]
                rows, w = (META, 1) if job == "meta" else (P, 4)
                v.wait_ge(sd_done, n + 1)
                v.reciprocal(rcol[0:rows, n, 0:w], sd[0:rows, 0:w]).then_inc(rcol_done, 1)

            def operand(entry):
                o, r = OPN[entry], R2N[entry]

                def update(k):
                    if k >= 2:
                        v.wait_ge(x_new, KT * (r - 1) + k - 1)
                    step(stt(tmp[:, k % 2], M[:, k], M_GAIN[entry](k), PS[:, RB], ALU.mult, ALU.mult))
                    tt(X[:, k], X[:, k], tmp[:, k % 2], ALU.add).then_inc(x_new, 1)

                def split(k):
                    v.wait_ge(xh, KT * o + k + 1)
                    stt(XL[:, k], X[:, k], ENTRY_GAIN[entry](k), f(XH[:, k]), ALU.mult, ALU.subtract).then_inc(xl, 1)

                if entry in M_GAIN:
                    v.wait_ge(rb_done, JOB["m" + entry[1]] + 1)
                    for k in range(KT + 1):
                        if k < KT:
                            update(k)
                        if k >= 1:
                            split(k - 1)
                else:
                    for k in range(KT):
                        split(k)
                ssq_n[0] += KT - 1
                factor(entry)

            def scaled(dst, T, done, rows=P):
                v.wait_ge(blocks_done, done)
                sig(tt(dst, PS[0:rows, T % 4], r2[0:rows, :], ALU.mult), bank_free, T + 1)

            def angle(i, shift):
                step(ts(turns[:], ang[:], 0.15915494309189535, ALU.mult, shift, ALU.add))
                step(ts(turns[:], turns[:], 12582912.0, ALU.add, -12582912.0, ALU.add))
                for part in (6.28125, 0.0019350051879882812, 3.019916050461616e-07):
                    step(stt(trig[:, i], turns[:], -part, (ang if part > 6 else trig[:, i])[:], ALU.mult, ALU.add))
                if shift:
                    step(ts(trig[:, i], trig[:, i], 1.5707963267948966, ALU.add))
                sig(ts(trig[:, i], trig[:, i], 3.1415925, ALU.min, -3.1415925, ALU.max), angles, i + 1)

            operand("x0")

            T0, n0 = TILE0["w_in"], BLOCK0["w_in"]
            v.wait_ge(r2_done, 1)

            def latent(i, squared):
                scaled(lat[:, i], T0 + i, n0 + i + 1)
                if squared:
                    square_latent(i)

            def square_latent(i):
                step(tt(sqb[:, 0], lat[:, i], lat[:, i], ALU.mult))
                add_squares(sqb[:, 0])

            def norm_latent(i, g):
                step(stt(lat[:, i], lat[:, i], g, PS[:, RB], ALU.mult, ALU.mult))
                step(v.tensor_copy(LH[:, i], lat[:, i]))
                sig(tt(LL[:, i], lat[:, i], f(LH[:, i]), ALU.subtract), lat_done, i + 1)

            def rotate(x1, x2, free1=None, free2=None):
                step(tt(sqb[:, 0], x1, trig[:, 0], ALU.mult))
                step(tt(sqb[:, 1], x2, trig[:, 1], ALU.mult))
                step(tt(sqb[:, 0], sqb[:, 0], sqb[:, 1], ALU.subtract))
                step(v.tensor_copy(rope_h[:, 0], sqb[:, 0]))
                step(tt(rope_l[:, 0], sqb[:, 0], f(rope_h[:, 0]), ALU.subtract))
                step(tt(sqb[:, 0], x2, trig[:, 0], ALU.mult))
                last = tt(sqb[:, 1], x1, trig[:, 1], ALU.mult)
                sig(last, bank_free, free1) if free1 else step(last)
                last = tt(sqb[:, 0], sqb[:, 0], sqb[:, 1], ALU.add)
                sig(last, bank_free, free2) if free2 else step(last)
                step(v.tensor_copy(rope_h[:, 1], sqb[:, 0]))

            clear_ssq("q_lat")
            for i in range(3):
                latent(i, True)
            latent(3, False)
            v.wait_ge(pos_in, 16)
            step(v.tensor_copy(ang[:], pos_i[:]))
            step(ts(ang[:], ang[:], col("inv_freq"), ALU.mult))
            factor("q_lat")
            angle(0, 0.25)
            latent(4, False)
            angle(1, 0.0)
            scaled(tmp[:, 0], T0 + 5, n0 + 6)
            v.wait_ge(rb_done, JOB["q_lat"] + 1)
            for i in range(3):
                norm_latent(i, col("q_norm", i))
            clear_ssq("kv_lat")
            square_latent(3)
            square_latent(4)
            scaled(tmp[:, 1], T0 + 6, n0 + 7)
            scaled(gate_c[:, 0], T0 + 7, n0 + 8)
            factor("kv_lat")
            scaled(gate_c[:, 1], T0 + 8, n0 + 9)
            v.wait_ge(rb_done, JOB["kv_lat"] + 1)
            for i in range(2):
                norm_latent(3 + i, col("kv_norm", i))
            v.wait_ge(trig_done, 1)
            rotate(tmp[:, 0], tmp[:, 1])
            sig(tt(rope_l[:, 1], sqb[:, 0], f(rope_h[:, 1]), ALU.subtract), rope_done, 1)
            v.wait_ge(meta_in, 16)
            step(tt(meta_n[:], meta[:], meta[:], ALU.mult))
            v.wait_ge(stat_done, JOB["meta"])
            ssq_n[0] += 1
            sig(v.tensor_reduce(ssq[:, 0:META], meta_n[:].rearrange("p k t -> p t k"), AX.X, ALU.add),
                ssq_adds, ssq_n[0])
            scaled(gate_c[:, 2], T0 + 9, n0 + 10)
            scaled(gate_c[:, 3], T0 + 10, n0 + 11)
            step(v.memset(gated[:, :, 0:1], 0.0))
            step(v.memset(gated[:, :, S + 1:S + 2], 0.0))
            for i in range(4):
                scaled(sqb[:, 0], T0 + 11 + i, n0 + 12 + i)
                step(tt(gated[:, i, 1:S + 1], sqb[:, 0], gate_c[:, i], ALU.mult))
                tap = [col("sc", 4 * t + i) for t in range(3)]
                step(ts(y_conv[:, i], gated[:, i, 0:S], tap[0], ALU.mult))
                step(stt(y_conv[:, i], gated[:, i, 1:S + 1], tap[1], y_conv[:, i], ALU.mult, ALU.add))
                step(stt(y_conv[:, i], gated[:, i, 2:S + 2], tap[2], y_conv[:, i], ALU.mult, ALU.add))
                if i == 2:
                    factor("meta")
            v.wait_ge(rb_done, JOB["meta"] + 1)
            for k in range(KT):
                step(stt(meta_n[:, k], meta[:, k], col("norm1_2", k), PS[:, RB, 0:META], ALU.mult, ALU.mult))
            step(v.tensor_copy(meta_h[:], meta_n[:]))
            sig(tt(meta_l[:], meta_n[:], f(meta_h[:]), ALU.subtract), meta_split, 1)
            for i in range(4):
                scaled(sqb[:, 0], T0 + 15 + i, n0 + 16 + i)
                sig(tt(y_conv[:, i], y_conv[:, i], sqb[:, 0], ALU.mult), y_ready, i + 1)
            lo_n = [0]

            def ev_sub(dst, src, hi_part):
                lo_n[0] += 1
                v.wait_ge(ev_hi, lo_n[0])
                return tt(dst, src, f(hi_part), ALU.subtract)

            def heads_lo(H, L, phase, t):
                b = (TILE0[phase] + t + (2 if phase == "up_q" else 0)) % 4
                ev_sub(L[0:NOPE, 2 * t], PS[0:NOPE, b], H[0:NOPE, 2 * t]).then_inc(ev_lo, 1)
                ev_sub(L[NOPE:P, 2 * t + 1], PS[NOPE:P, b], H[NOPE:P, 2 * t + 1]).then_inc(bank_free, 1)

            T = TILE0["up_q"]
            v.wait_ge(blocks_done, BLOCK0["up_q"] + 1)
            v.wait_ge(kpe_in, 16 * K_ROPE_DMAS)
            rotate(PS[:, T % 4], PS[:, (T + 1) % 4], T + 1, T + 2)
            sig(tt(rope_l[:, 1], sqb[:, 0], f(rope_h[:, 1]), ALU.subtract), rope_done, 2)
            for t in range(4):
                heads_lo(QH, QL, "up_q", t)
            for t in range(4):
                heads_lo(KH, KL, "up_kn", t)
            for t in range(4):
                ev_sub(VL[:, t], PS[:, (TILE0["up_v"] + t) % 4], VH[:, t]).then_inc(bank_free, 1)
            for t in range(4):
                ev_sub(XL[:, t], y_conv[:, t], XH[:, t]).then_inc(ev_lo, 1)

            def attention(layer):
                U0, H0 = layer * UNITS, layer * HEADS
                for s in range(UNITS + 7):
                    if s < UNITS:
                        v.wait_ge(s_done, U0 + s + 1)
                        v.tensor_reduce(cols[:, s % 4, 0:1], score_area(layer, s), AX.X, ALU.max,
                                        negate=True).then_inc(neg_max, 1)
                    u = s - 1
                    if 0 <= u < UNITS:
                        v.wait_ge(exp_done, U0 + u + 1)
                        v.reciprocal(cols[:, u % 4, 2:3], cols[:, u % 4, 1:2]).then_inc(inv_sum, 1)
                    u = s - 4
                    if 0 <= u < UNITS:
                        pair, q = u // 2, slice(P * (u % 2), P * (u % 2) + P)
                        v.wait_ge(ph_done, U0 + u + 1)
                        main, small = turned_area(layer, u)
                        if layer == 0:
                            tt(PL[:, pair % 2, :, q], main, f(PH[:, pair % 2, :, q]), ALU.subtract).then_inc(pl_done, 1)
                        else:
                            i = u % 4
                            step(tt(P2L[0:META, pair % 2, 4, q], small, f(P2H[0:META, pair % 2, 4, q]), ALU.subtract))
                            tt(P2L[:, pair % 2, 0:i + 1, q], main, f(P2H[:, pair % 2, 0:i + 1, q]),
                               ALU.subtract).then_inc(pl_done, 1)
                    if layer == 1 and s % P_OUT_STEPS == 2 and s // P_OUT_STEPS < 4:
                        t = s // P_OUT_STEPS
                        v.wait_ge(p_out_h, t + 1)
                        tt(XL[:, 4 + t], p_out(t), f(XH[:, 4 + t]), ALU.subtract).then_inc(p_out_l, 1)
                    if s >= 9 and s % 4 == 1:
                        h = (s - 9) // 4
                        rows = slice(64 * (h % 2), 64 * (h % 2) + 64)
                        y = (4 if layer == 0 else 0) + h // 2
                        v.wait_ge(yh_done, H0 + h + 1)
                        tt(XL[rows, y], PS[rows, result_bank(layer, h)], f(XH[rows, y]), ALU.subtract).then_inc(yl_done, 1)

            attention(0)

            def outputs(phase, job, bias=None):
                v.wait_ge(stat_done, JOB[job])
                for m in range(KT):
                    T = TILE0[phase] + m
                    v.wait_ge(blocks_done, BLOCK0[phase] + m + 1)
                    if bias:
                        sig(ts(M[:, m], PS[:, T % 4], bias(m), ALU.add), bank_free, T + 1)
                    else:
                        sig(v.tensor_copy(M[:, m], PS[:, T % 4]), bank_free, T + 1)
                    if m == 0:
                        ssq_n[0] += 1
                        sig(tt(ssq[:], M[:, m], M[:, m], ALU.mult), ssq_adds, ssq_n[0])
                    else:
                        step(tt(tmp[:, 0], M[:, m], M[:, m], ALU.mult))
                        add_squares(tmp[:, 0])
                factor(job)

            outputs("w_out", "m1")

            def mlp(layer, entry, out_job):
                operand(entry)
                v.wait_ge(r2_done, R2N[entry] + 1)
                for c in range(NCHUNK):
                    phase = f"mlp{layer}_up{c}"
                    T0, n0 = TILE0[phase], BLOCK0[phase]
                    base = chain[0]
                    h0 = (layer * NCHUNK + c) * CHUNK
                    with v.Fori(0, CHUNK // 4, 1) as g:
                        for j in range(4):
                            T = g * 4 + (T0 + j)
                            own = g * 8 + (base + 2 * j)
                            v.wait_ge(blocks_done, g * 4 + (n0 + j + 1))
                            tt(tmp[:, 0], PS[:, (T0 + j) % 4], r2[:], ALU.mult).then_inc(bank_free, 1)
                            v.wait_ge(bank_free, T + 1)
                            stt(tmp[:, 1], tmp[:, 0], 0.0, tmp[:, 0], ALU.max, ALU.mult).then_inc(dve, 1)
                            v.wait_ge(dve, own + 1)
                            v.tensor_copy(HH[:, g * 4 + j], tmp[:, 1]).then_inc(dve, 1)
                            v.wait_ge(dve, own + 2)
                            tt(HL[:, g * 4 + j], tmp[:, 1], f(HH[:, g * 4 + j]), ALU.subtract).then_inc(hid, 1)
                            v.wait_ge(hid, g * 4 + (h0 + j + 1))
                    chain[0] += 2 * CHUNK
                    phase = f"mlp{layer}_down{c}"
                    T0, n0 = TILE0[phase], BLOCK0[phase]
                    last = c == NCHUNK - 1
                    if last:
                        clear_ssq(out_job)
                    base, sq0 = chain[0], ssq_n[0]
                    with v.Fori(0, KT // 4, 1) as g:
                        for j in range(4):
                            m = g * 4 + j
                            v.wait_ge(blocks_done, g * 8 + (n0 + 2 * j + 2))
                            b = (T0 + j) % 4
                            if c == 0:
                                v.tensor_copy(M[:, m], PS[:, b]).then_inc(bank_free, 1)
                            else:
                                tt(M[:, m], M[:, m], PS[:, b], ALU.add).then_inc(bank_free, 1)
                            v.wait_ge(bank_free, g * 4 + (T0 + j + 1))
                            if last:
                                tt(tmp[:, 0], M[:, m], M[:, m], ALU.mult).then_inc(dve, 1)
                                v.wait_ge(dve, g * 4 + (base + j + 1))
                                tt(ssq[:], ssq[:], tmp[:, 0], ALU.add).then_inc(ssq_adds, 1)
                                v.wait_ge(ssq_adds, g * 4 + (sq0 + j + 1))
                    if last:
                        chain[0] += KT
                        ssq_n[0] += KT
                factor(out_job)

            mlp(0, "x1", "m2")

            operand("x2")
            v.wait_ge(r2_done, R2N["x2"] + 1)
            T0, n0 = TILE0["pw1"], BLOCK0["pw1"]
            for side in (slice(0, PAD), slice(PAD + S, UW)):
                step(v.memset(U[:, :, side], 0.0))
            for kind, j in PW1:
                T, done = T0 + PW1_TILE[(kind, j)], n0 + PW1_BLOCK[(kind, j)] + 1
                b = j % 2
                if kind == "a":
                    scaled(tmp[:, 0], T, done)
                elif kind == "g":
                    v.wait_ge(blocks_done, done)
                    tt(tmp[:, 1], PS[:, T % 4], r2[:], ALU.mult).then_inc(gate_z, 1)
                    v.wait_ge(gate_s, j + 1)
                    if j >= 2:
                        v.wait_ge(uh_done, j - 1)
                        v.wait_ge(ul_done, j - 1)
                    sig(stt(U[:, b, PAD:PAD + S], tmp[:, 0], col("b_pw1", j), sqb[:, 0], ALU.add, ALU.mult), u_done, j + 1)
                    for t in range(PE_TAPS, PE_TAPS + DVE_TAPS):
                        a = acc[:, b, t % 2]
                        w, src = col("w_dw", j * TAPS + t), U[:, b, t:t + S]
                        if t < PE_TAPS + 2:
                            ins = ts(a, src, w, ALU.mult)
                        else:
                            v.wait_ge(dve, chain[0] - (1 if t > PE_TAPS + 2 else 0))
                            ins = stt(a, src, w, a, ALU.mult, ALU.add)
                        if t == PE_TAPS:
                            sig(ins, bank_free, T + 1)
                        elif t == PE_TAPS + DVE_TAPS - 1:
                            ins.then_inc(dve_taps, 1)
                        else:
                            chain[0] += 1
                            ins.then_inc(dve, 1)
                else:
                    v.wait_ge(blocks_done, done)
                    v.wait_ge(dve_taps, j + 1)
                    sig(stt(conv[:, j], PS[:, T % 4], col("b_dw", j), acc[:, b, 0], ALU.add, ALU.add), bank_free, T + 1)
                    v.wait_ge(taps_done, j + 1)
                    sig(tt(conv[:, j], conv[:, j], acc_p[:, b], ALU.add), conv_done, j + 1)
            clear_ssq("ln")
            v.wait_ge(mean_done, 1)
            for k in range(KT + 1):
                if k < KT:
                    stt(conv[:, k], PS[:, HB], -1.0 / D, conv[:, k], ALU.mult, ALU.add).then_inc(centred, 1)
                if k:
                    v.wait_ge(squares, SQUARES["ln"] + k)
                    add_squares(sqb[:, (k - 1) % 2])
            factor("ln")
            v.wait_ge(rb_done, JOB["ln"] + 1)
            for k in range(KT + 1):
                if k < KT:
                    if k >= 2:
                        v.wait_ge(ln_s, k - 1)
                    stt(tmp[:, k % 2], conv[:, k], col("ln_g", k), PS[:, RB], ALU.mult, ALU.mult).then_inc(ln_z, 1)
                if k:
                    v.wait_ge(xh, KT * OPN["ln"] + k)
                    tt(XL[:, k - 1], sqb[:, (k - 1) % 2], f(XH[:, k - 1]), ALU.subtract).then_inc(xl, 1)
            outputs("pw2", "m3", bias=lambda m: col("b_pw2", m))
            mlp(1, "x3", "m4")

            operand("x4")
            v.wait_ge(r2_done, R2N["x4"] + 1)
            T0, n0 = TILE0["w_in_2"], BLOCK0["w_in_2"]

            def head_in(e, phase, i):
                T, done = TILE0[phase] + i, BLOCK0[phase] + i + 1
                t = head_t[:, e % 4]
                if e < 4:
                    out = t[:, 0:S]
                else:
                    v.wait_ge(blocks_done, done)
                    step(v.tensor_copy(t[:, 0:META], PS[:, META_BANK, 0:META]))
                    out = t[:, META:L2]
                v.wait_ge(blocks_done, done)
                sig(tt(out, PS[:, T % 4], r2[:], ALU.mult), bank_free, T + 1)

            def head_norm(e):
                keys = e >= 4
                v.wait_ge(hsd, e + 1)
                step(v.reciprocal(hcol[:, 1, 0:8], hcol[:, 0, 0:8]))
                ins = v.tensor_copy(hexp[:].rearrange("p c (h j) -> p (c h) j", h=2),
                                    hcol[:, 1, 0:8].unsqueeze(2).broadcast_to((P, 8, HD)))
                if keys:
                    step(ins)
                    step(v.reciprocal(hcol[0:META, 1, 8:10], hcol[0:META, 0, 8:10]))
                    ins = v.tensor_copy(meta_x[:].rearrange("p (h j) -> p h j", h=2),
                                        hcol[0:META, 1, 8:10].unsqueeze(2).broadcast_to((META, 2, HD)))
                ins.then_inc(hexp_done, 1)
                v.wait_ge(hb_done, e + 1)
                t = head_t[:, e % 4]
                g = col("k_norm_2" if keys else "q_norm_2")
                tokens = t[:, META:L2] if keys else t[:, 0:S]
                step(stt(tokens, tokens, g, PS[:, HB], ALU.mult, ALU.mult))
                if keys:
                    step(stt(t[:, 0:META], t[:, 0:META], g, PS[:, STAT, 32:32 + META], ALU.mult, ALU.mult))
                    dh, dl, w = K2H[:, e - 4], K2L[:, e - 4], L2
                else:
                    dh, dl, w = Q2H[:, e], Q2L[:, e], S
                step(v.tensor_copy(dh, t[:, 0:w]))
                sig(tt(dl, t[:, 0:w], f(dh), ALU.subtract), heads_done, e + 1)

            def log_forget():
                T, done = T0 + 4, n0 + 5
                bias = vec[0:HEADS, COL["b_fgate"]:COL["b_fgate"] + 1]
                v.wait_ge(blocks_done, done)
                step(ts(logf[:, 0, 0:META], PS[0:HEADS, META_BANK, 0:META], bias, ALU.add))
                scaled(logf[:, 0, META:L2], T, done, rows=HEADS)
                step(ts(logf[:, 0, META:L2], logf[:, 0, META:L2], bias, ALU.add))
                sig(stt(logf[:, 1], logf[:, 0], -1.0, logf[:, 0], ALU.mult, ALU.max), fz, 1)

            def prefix_sums():
                v.wait_ge(fexp, 1)
                step(stt(logf[:, 2], logf[:, 0], 0.0, logf[:, 1], ALU.min, ALU.subtract))
                step(v.memset(logf[:, 1], 1.0))
                step(v.tensor_tensor_scan(logf[:, 0], logf[:, 1], logf[:, 2], 0.0, ALU.mult, ALU.add))
                step(v.tensor_copy(cum_h[:], logf[:, 0]))
                step(v.memset(f(CQ[:]), -1.0))
                step(v.memset(f(CK[:]), 1.0))
                sig(tt(cum_l[:], logf[:, 0], f(cum_h[:]), ALU.subtract), cum_done, 1)

            def pool_tile(i):
                T, done = T0 + 5 + i, n0 + 6 + i
                v.wait_ge(blocks_done, done)
                step(v.tensor_copy(u2[:, 0:META], PS[:, META_BANK, 0:META]))
                scaled(u2[:, META:L2], T, done)
                src, w = u2, 1
                for d in range(i + 1):
                    dst = pool_a[:, d % 2]
                    a = u2[:] if d == 0 else pool_a[:, (d - 1) % 2]
                    step(tt(dst[:, 2 * w - 1:L2], a[:, 2 * w - 1:L2], a[:, w - 1:L2 - w], ALU.add))
                    w *= 2
                assert w == WINDOWS[i]
                sig(stt(pooled[:, i], pool_a[:, i % 2, META:L2], 1.0 / w, u2[:, META:L2], ALU.mult, ALU.subtract),
                    pooled_done, i + 1)

            def pool_lo_part(i):
                v.wait_ge(pool_hi, i + 1)
                tt(pool_l[:, i], pooled[:, i], f(pool_h[:, i]), ALU.subtract).then_inc(pool_lo, 1)

            for e in range(4):
                head_in(e, "w_in_2", e)
            head_norm(0)
            head_norm(1)
            log_forget()
            head_norm(2)
            pool_tile(0)
            prefix_sums()
            head_norm(3)
            for i in range(1, 4):
                pool_tile(i)
                pool_lo_part(i - 1)
            pool_lo_part(3)
            head_in(4, "w_in_2", 9)
            for i in range(4):
                T = TILE0["pool"] + i
                v.wait_ge(blocks_done, BLOCK0["pool"] + 1)
                sig(ts(p_out(i), PS[:, T % 4], col("pool_scale", i), ALU.mult), bank_free, T + 1)
            head_norm(4)
            for e in range(5, 8):
                head_in(e, "w_in_2b", e - 5)
                head_norm(e)
            for t in range(4):
                T = TILE0["w_in_2b"] + 3 + t
                lo_n[0] += 1
                v.wait_ge(ev_hi, lo_n[0])
                sig(stt(V2L[:, t], PS[:, T % 4], rcol[:, JOB["x4"], t:t + 1], f(V2H[:, t]), ALU.mult, ALU.subtract),
                    bank_free, T + 1)
            sig(ev_sub(V2L[0:META, 4], PS[0:META, META_BANK], V2H[0:META, 4]), v_meta_free, 1)
            attention(1)

            for m in range(KT):
                T = TILE0["w_out_2"] + m
                v.wait_ge(blocks_done, BLOCK0["w_out_2"] + m + 1)
                tt(X[:, m], X[:, m], PS[:, T % 4], ALU.add).then_inc(bank_free, 1)
            operand("x5")

            v.wait_ge(r2_done, R2N["x5"] + 1)
            T0, n0 = TILE0["ffn_up"], BLOCK0["ffn_up"]
            base, h0 = chain[0], 2 * NCHUNK * CHUNK
            with v.Fori(0, HT2 // 2, 1) as g:
                for j in range(2):
                    T = g * 4 + (T0 + 2 * j)
                    own = g * 4 + (base + 2 * j)
                    p = g * 2 + j
                    v.wait_ge(blocks_done, g * 4 + (n0 + 2 * j + 1))
                    tt(tmp[:, 0], PS[:, (T0 + 2 * j) % 4], r2[:], ALU.mult).then_inc(gate_z, 1)
                    v.wait_ge(blocks_done, g * 4 + (n0 + 2 * j + 2))
                    tt(tmp[:, 1], PS[:, (T0 + 2 * j + 1) % 4], r2[:], ALU.mult).then_inc(bank_free, 1)
                    v.wait_ge(bank_free, T + 1)
                    v.wait_ge(gate_s, p + (KT + 1))
                    tt(tmp[:, 1], tmp[:, 1], sqb[:, 0], ALU.mult).then_inc(bank_free, 1)
                    v.wait_ge(bank_free, T + 2)
                    v.tensor_copy(HH[:, p], tmp[:, 1]).then_inc(dve, 1)
                    v.wait_ge(dve, g * 2 + (base + j + 1))
                    tt(HL[:, p], tmp[:, 1], f(HH[:, p]), ALU.subtract).then_inc(hid, 1)
                    v.wait_ge(hid, p + (h0 + 1))
            chain[0] += HT2
            T0, n0 = TILE0["ffn_down"], BLOCK0["ffn_down"]
            for m in range(KT):
                v.wait_ge(blocks_done, n0 + 3 * m + 3)
                tt(X[:, m], X[:, m], PS[:, (T0 + m) % 4], ALU.add).then_inc(bank_free, 1)

        @block.tensor
        def _(pe):
            def products(out, wa, wb, xa, xb, start, stop):
                pe.matmul(out, wa, xa, start=start, stop=False)
                pe.matmul(out, wa, xb, start=False, stop=False)
                return pe.matmul(out, wb, xa, start=False, stop=stop)

            def weight(n, k):
                return wh[:, n % RING, k], wl[:, n % RING, k]

            def keep_busy(count, out):
                for _ in range(count):
                    pe.matmul(out, ident_r[:], ident_r[:].unsqueeze(1).broadcast_to((P, out.shape[-1] // P, P)),
                              start=True, stop=True)

            def open_block(n):
                pe.wait_ge(w_lo, n + 1)

            def open_tile(T):
                if T >= 4:
                    pe.wait_ge(bank_free, T - 3)

            def stat(job):
                n = JOB[job]
                pe.wait_ge(ssq_adds, SSQ_ADDS[n])
                if n:
                    pe.wait_ge(sd_done, n)
                if job == "meta":
                    pe.matmul(PS[0:META, STAT, 0:1], ssq[:, 0:META], ones[:, 0:1], start=True, stop=True).then_inc(stat_done, 1)
                    return
                for j in range(4):
                    ins = pe.matmul(PS[:, STAT, j:j + 1], ssq[:, j * P:(j + 1) * P], ones[:, 0:1], start=True, stop=True)
                ins.then_inc(stat_done, 1)

            def spread(job):
                n = JOB[job]
                pe.wait_ge(rcol_done, n + 1)
                if job == "meta":
                    pe.matmul(PS[:, RB, 0:META], rcol[0:META, n, 0:1].broadcast_to((META, P)), ident[0:META, 0:META],
                              start=True, stop=True).then_inc(rb_done, 1)
                    return
                for j in range(4):
                    ins = pe.matmul(PS[:, RB, j * P:(j + 1) * P], rcol[:, n, j:j + 1].broadcast_to((P, P)), ident[:],
                                    start=True, stop=True)
                ins.then_inc(rb_done, 1)

            def tile(n, T, hooks={}, meta_out=None):
                open_block(n)
                open_tile(T)
                for k in range(KT):
                    if k in hooks:
                        hooks[k]()
                    ins = products(PS[:, T % 4], *weight(n, k), XH[:, k], XL[:, k], k == 0, k == KT - 1)
                if meta_out is not None:
                    pe.wait_ge(bank_free, meta_out)
                    for k in range(KT):
                        ins = products(PS[:, META_BANK, 0:META], *weight(n, k), meta_h[:, k], meta_l[:, k],
                                       k == 0, k == KT - 1)
                ins.then_inc(blocks_done, 1)

            def enter(phase, operand, hook_job=None):
                n0, T0, x0 = BLOCK0[phase], TILE0[phase], KT * OPN[operand]
                for t in range(3):
                    open_block(n0 + t)
                    open_tile(T0 + t)
                for k in range(KT):
                    pe.wait_ge(xh, x0 + k + 1)
                    pe.wait_ge(xl, x0 + k + 1)
                    for t in range(3):
                        ins = products(PS[:, (T0 + t) % 4], *weight(n0 + t, k), XH[:, k], XL[:, k], k == 0, k == KT - 1)
                        if k == KT - 1:
                            ins.then_inc(blocks_done, 1)
                hooks = {1: lambda: stat(hook_job), 5: lambda: spread(hook_job)} if hook_job else {}
                tile(n0 + 3, T0 + 3, hooks)

            def norm_out(job, before=W_STAT, after=W_UPDATE):
                keep_busy(before, PS[:, META_BANK])
                stat(job)
                keep_busy(W_FACTOR, PS[:, META_BANK])
                spread(job)
                keep_busy(after, PS[:, META_BANK])

            pe.wait_ge(consts, NCONST)
            enter("w_in", "x0", "x0")

            def spread_kv():
                pe.wait_ge(lat_done, 3)
                spread("kv_lat")

            def spread_meta():
                pe.wait_ge(lat_done, 5)
                spread("meta")

            hooks = {5: {4: lambda: stat("q_lat")}, 6: {4: lambda: spread("q_lat")},
                     8: {4: lambda: stat("kv_lat")}, 9: {4: lambda: spread_kv()},
                     11: {4: lambda: stat("meta")}, 14: {6: lambda: spread_meta()}}
            for t in range(4, 19):
                tile(t, t, hooks.get(t, {}))

            def up(n, slots, T, first, nk):
                open_tile(T)
                for k in range(nk):
                    ins = products(PS[:, T % 4], *weight(n, slots + k), LH[:, first + k], LL[:, first + k],
                                   k == 0, k == nk - 1)
                return ins

            pe.wait_ge(lat_done, 5)
            n0, T0 = BLOCK0["up_q"], TILE0["up_q"]
            for b in range(3):
                open_block(n0 + b)
                up(n0 + b, 0, T0 + 2 * b, 0, 3)
                up(n0 + b, 3, T0 + 2 * b + 1, 0, 3).then_inc(blocks_done, 1)
            n0, T0 = BLOCK0["up_kn"], TILE0["up_kn"]
            open_block(n0)
            for t in range(4):
                ins = up(n0, 2 * t, T0 + t, 3, 2)
            ins.then_inc(blocks_done, 1)
            n0, T0 = BLOCK0["up_v"], TILE0["up_v"]
            open_block(n0)
            for t in range(4):
                open_tile(T0 + t)
                q = slice(t * P, (t + 1) * P)
                for k in range(2):
                    w = [x[:, n0 % RING, 4 * k:4 * k + 4].rearrange("p s m -> p (s m)") for x in (wh, wl)]
                    ins = products(PS[:, (T0 + t) % 4], LH[:, 3 + k, q], LL[:, 3 + k, q], *w, k == 0, k == 1)
            ins.then_inc(blocks_done, 1)

            def attention(layer):
                U0, H0 = layer * UNITS, layer * HEADS

                def scores(u):
                    h, i = divmod(u, 4)
                    q = slice(i * P, (i + 1) * P)
                    out = score_area(layer, u)
                    ring = 3 if layer == 0 else 2
                    if u >= ring:
                        pe.wait_ge(exp_done, U0 + u - ring + 1)
                    if layer == 0:
                        rows = slice(0, NOPE + ROPE) if h % 2 == 0 else slice(0, P)
                        products(out, QH[rows, h, q], QL[rows, h, q], KH[rows, h], KL[rows, h],
                                 True, True).then_inc(s_done, 1)
                        return
                    rows = slice(64 * (h % 2), 64 * (h % 2) + 64)
                    pair, a, b = h // 2, 32 * (h % 4), h // 4
                    w = P * (i + 1) + META
                    qh, ql, kh, kl = (x[rows, pair] for x in (Q2H, Q2L, K2H, K2L))
                    for lo, hi_ in ((0, w),) if i < 3 else ((0, w - P), (w - P, w)):
                        part = out[:, lo:hi_]
                        products(part, qh[:, q], ql[:, q], kh[:, lo:hi_], kl[:, lo:hi_], True, False)
                        ins = pe.matmul(part, CQ[a:a + 4, b, q], CK[a:a + 4, b, lo:hi_], start=False, stop=hi_ < w)
                    ins = pe.matmul(out[:, w - P:w], ident_r[:], mask_r[:], start=False, stop=True)
                    ins.then_inc(s_done, 1)

                def turn(u):
                    ring = 3 if layer == 0 else 2
                    if u >= ring:
                        pe.wait_ge(pl_done, U0 + u - ring + 1)
                    pe.wait_ge(p_done, U0 + u + 1)
                    main, small = turned_area(layer, u)
                    if layer == 0:
                        for k in range(4):
                            ins = pe.transpose(main[:, k], prob[:, u % 4, k * P:(k + 1) * P], ident[:])
                    else:
                        p = prob2[:, u % 3]
                        pe.transpose(small, p[:, 0:META], ident[:])
                        for k in range(u % 4 + 1):
                            ins = pe.transpose(main[:, k], p[:, META + k * P:META + (k + 1) * P], ident[:])
                    ins.then_inc(t_done, 1)

                def values(pair):
                    h, half = divmod(pair, 2)
                    ring = 2 if layer == 0 else 1
                    if half == 0 and h >= ring:
                        pe.wait_ge(yl_done, H0 + h - ring + 1)
                    cols_v = slice(h // 2 * P, h // 2 * P + P)
                    o = PS[:, result_bank(layer, h), half * 2 * P:(half + 1) * 2 * P]
                    keep_busy(W_VALUES[layer], o)
                    pe.wait_ge(pl_done, U0 + 2 * pair + 2)
                    if layer == 0:
                        for k in range(4):
                            ins = products(o, VH[:, k, cols_v], VL[:, k, cols_v], PH[:, pair % 2, k],
                                           PL[:, pair % 2, k], k == 0, k == 3)
                    else:
                        ph, pl = P2H[:, pair % 2], P2L[:, pair % 2]
                        products(o, V2H[0:META, 4, cols_v], V2L[0:META, 4, cols_v], ph[0:META, 4], pl[0:META, 4],
                                 True, False)
                        last = 2 * half + 1
                        for k in range(last + 1):
                            q = slice(P if k == last else 0, 2 * P)
                            ins = products(o[:, q], V2H[:, k, cols_v], V2L[:, k, cols_v], ph[:, k, q], pl[:, k, q],
                                           False, k == last)
                    ins.then_inc(pv_done, 1)

                for s in range(UNITS + 5):
                    if s < UNITS:
                        scores(s)
                    if s >= 6 and s % 2 == 0:
                        values((s - 6) // 2)
                    if 0 <= s - 3 < UNITS:
                        turn(s - 3)

            pe.wait_ge(bank_free, TILE0["w_out"])
            pe.wait_ge(kpe_in, 16 * K_ROPE_DMAS)
            pe.wait_ge(qpe_in, 16 * Q_ROPE_DMAS)
            pe.wait_ge(rows_zero, 4)
            attention(0)
            n0, T0 = BLOCK0["w_out"], TILE0["w_out"]
            pe.wait_ge(ev_lo, 12)
            pe.wait_ge(yl_done, HEADS)
            for m in range(KT):
                tile(n0 + m, T0 + m)
            norm_out("m1")

            def mlp(layer, entry, out_job):
                for c in range(NCHUNK):
                    n0, T0 = BLOCK0[f"mlp{layer}_up{c}"], TILE0[f"mlp{layer}_up{c}"]
                    if c == 0:
                        enter(f"mlp{layer}_up0", entry, entry)
                    with pe.Fori(1 if c == 0 else 0, CHUNK // 4, 1) as g:
                        for j in range(4):
                            pe.wait_ge(w_lo, g * 4 + (n0 + j + 1))
                            pe.wait_ge(bank_free, g * 4 + (T0 + j - 3))
                            for k in range(KT):
                                ins = products(PS[:, (T0 + j) % 4], *weight(n0 + j, k), XH[:, k], XL[:, k],
                                               k == 0, k == KT - 1)
                            ins.then_inc(blocks_done, 1)
                    h0 = (layer * NCHUNK + c) * CHUNK
                    n0, T0 = BLOCK0[f"mlp{layer}_down{c}"], TILE0[f"mlp{layer}_down{c}"]
                    with pe.Fori(0, KT // 4, 1) as g:
                        for j in range(4):
                            pe.wait_ge(bank_free, g * 4 + (T0 + j - 3))
                            for b in range(2):
                                pe.wait_ge(w_lo, g * 8 + (n0 + 2 * j + b + 1))
                                pe.wait_ge(hid, h0 + SLOTS * (b + 1))
                                for k in range(SLOTS):
                                    x = SLOTS * b + k
                                    ins = products(PS[:, (T0 + j) % 4], *weight(n0 + 2 * j + b, k), HH[:, x], HL[:, x],
                                                   x == 0, x == CHUNK - 1)
                                ins.then_inc(blocks_done, 1)
                norm_out(out_job)

            mlp(0, "x1", "m2")

            enter("pw1", "x2", "x2")
            n0, T0 = BLOCK0["pw1"], TILE0["pw1"]
            for kind, j in PW1[4:]:
                n, T = n0 + PW1_BLOCK[(kind, j)], T0 + PW1_TILE[(kind, j)]
                if kind != "c":
                    tile(n, T)
                    continue
                open_tile(T)
                pe.wait_ge(uh_done, j + 1)
                pe.wait_ge(ul_done, j + 1)
                for t in range(PE_TAPS):
                    if t % SLOTS == 0:
                        open_block(n + t // SLOTS)
                    ins = products(PS[:, T % 4], *weight(n + t // SLOTS, t % SLOTS), UH[:, j % 2, t:t + S],
                                   UL[:, j % 2, t:t + S], t == 0, t == PE_TAPS - 1)
                    if t % SLOTS == SLOTS - 1 or t == PE_TAPS - 1:
                        ins.then_inc(blocks_done, 1)
            keep_busy(W_MEAN, PS[:, META_BANK])
            pe.wait_ge(sum1_done, KT)
            pe.matmul(PS[:, HB], ones[:], sum1[:], start=True, stop=True).then_inc(mean_done, 1)
            norm_out("ln", W_CENTRE)
            enter("pw2", "ln")
            for m in range(4, KT):
                tile(BLOCK0["pw2"] + m, TILE0["pw2"] + m)
            norm_out("m3")
            mlp(1, "x3", "m4")

            enter("w_in_2", "x4", "x4")
            n0, T0 = BLOCK0["w_in_2"], TILE0["w_in_2"]

            def head_stat(e):
                keys = e >= 4
                pe.wait_ge(hsq, e + 1)
                if e == 0:
                    pe.wait_ge(sd_done, JOB["x4"] + 1)
                else:
                    pe.wait_ge(hsd, e)
                    pe.wait_ge(heads_done, e)
                two = headones[:, 0:P:HD]
                first = META if keys else 0
                if keys:
                    pe.matmul(PS[0:META, STAT, 8:10], head_q[:, 0:META], two, start=True, stop=True)
                for c in range(4):
                    ins = pe.matmul(PS[:, STAT, 2 * c:2 * c + 2], head_q[:, first + c * P:first + (c + 1) * P], two,
                                    start=True, stop=True)
                ins.then_inc(hstat, 1)

            def head_spread(e):
                pe.wait_ge(hexp_done, e + 1)
                if e >= 4:
                    pe.matmul(PS[:, STAT, 32:32 + META], meta_x[:], ident[0:META, 0:META], start=True, stop=True)
                for c in range(4):
                    ins = pe.matmul(PS[:, HB, c * P:(c + 1) * P], hexp[:, c], ident[:], start=True, stop=True)
                ins.then_inc(hb_done, 1)

            pe.wait_ge(meta_split, 1)
            head = lambda e: (lambda: head_stat(e), lambda: head_spread(e))
            norms = {4: {1: head(0)[0], 3: head(0)[1], 4: head(1)[0], 7: head(1)[1]},
                     5: {2: head(2)[0], 6: head(2)[1]}, 6: {3: head(3)[0], 7: head(3)[1]}}
            for i in range(4, 10):
                tile(n0 + i, T0 + i, norms.get(i, {}), meta_out=T0 + i)
            n1, T1 = BLOCK0["pool"], TILE0["pool"]
            open_block(n1)
            for i in range(4):
                open_tile(T1 + i)
                pe.wait_ge(pool_hi, i + 1)
                pe.wait_ge(pool_lo, i + 1)
                ins = products(PS[:, (T1 + i) % 4], *weight(n1, i), pool_h[:, i], pool_l[:, i], True, True)
            ins.then_inc(blocks_done, 1)
            n0, T0 = BLOCK0["w_in_2b"], TILE0["w_in_2b"]
            for i in range(3):
                tile(n0 + i, T0 + i, {4: head(4 + i)[0], 7: head(4 + i)[1]}, meta_out=T0 + i)
            open_tile(T0 + 6)
            for i in range(4):
                n = n0 + 3 + i
                open_block(n)
                if i == 1:
                    head_spread(7)
                for kk in range(2):
                    k = 2 * i + kk
                    w = [x[:, n % RING, 4 * kk:4 * kk + 4].rearrange("p s m -> p (s m)") for x in (wh, wl)]
                    if i == 0 and kk == 1:
                        head_stat(7)
                    for t in range(4):
                        q = slice(t * P, (t + 1) * P)
                        products(PS[:, (T0 + 3 + t) % 4], XH[:, k, q], XL[:, k, q], *w, k == 0, k == KT - 1)
                    ins = products(PS[0:META, META_BANK], meta_h[:, k], meta_l[:, k], *w, k == 0, k == KT - 1)
                ins.then_inc(blocks_done, 1)
            pe.wait_ge(decay_in, 16 * DECAY_DMAS)
            pe.wait_ge(consts_r, 2)
            pe.wait_ge(bank_free, T0 + 7)
            pe.wait_ge(v_meta_free, 1)
            pe.wait_ge(heads_done, 8)
            attention(1)
            n0, T0 = BLOCK0["w_out_2"], TILE0["w_out_2"]
            pe.wait_ge(p_out_l, 4)
            pe.wait_ge(yl_done, 2 * HEADS)
            for m in range(KT):
                tile(n0 + m, T0 + m)
            enter("ffn_up", "x5", "x5")
            n0, T0 = BLOCK0["ffn_up"], TILE0["ffn_up"]
            with pe.Fori(1, HT2 // 2, 1) as g:
                for j in range(4):
                    pe.wait_ge(w_lo, g * 4 + (n0 + j + 1))
                    pe.wait_ge(bank_free, g * 4 + (T0 + j - 3))
                    for k in range(KT):
                        ins = products(PS[:, (T0 + j) % 4], *weight(n0 + j, k), XH[:, k], XL[:, k], k == 0, k == KT - 1)
                    ins.then_inc(blocks_done, 1)
            h0 = 2 * NCHUNK * CHUNK
            n0, T0 = BLOCK0["ffn_down"], TILE0["ffn_down"]
            with pe.Fori(0, KT // 4, 1) as g:
                for j in range(4):
                    pe.wait_ge(bank_free, g * 4 + (T0 + j - 3))
                    for b in range(3):
                        pe.wait_ge(w_lo, g * 12 + (n0 + 3 * j + b + 1))
                        last = min(SLOTS * (b + 1), HT2)
                        pe.wait_ge(hid, h0 + last)
                        for x in range(SLOTS * b, last):
                            ins = products(PS[:, (T0 + j) % 4], *weight(n0 + 3 * j + b, x % SLOTS), HH[:, x], HL[:, x],
                                           x == 0, x == HT2 - 1)
                        ins.then_inc(blocks_done, 1)


def _tiles(w, k_tiles, m_tiles):
    full = np.zeros((k_tiles * P, m_tiles * P), w.dtype)
    full[:w.shape[0], :w.shape[1]] = w
    return full.reshape(k_tiles, P, m_tiles, P).transpose(2, 0, 1, 3)


def _pack_weights(even_w_in, even_w_uq, even_w_ukv, even_w_out, mlp_w1, mlp_w2, odd_w_pw1, odd_w_dw, odd_w_pw2,
                  w_in_2, w_pool_2, w_out_2, w_gate_2, w_up_2, w_down_2):
    out = np.zeros((NBLK, P, SLOTS, P), even_w_in.dtype)

    def put(n, slot, tiles):
        out[n, :, slot:slot + len(tiles)] = tiles.transpose(1, 0, 2)

    w = even_w_in[0]
    lat0 = 3 * SCW
    rope0 = lat0 + QR + KVR
    parts = [w[:, lat0:rope0]]
    for half in range(2):
        parts.append(np.tile(w[:, rope0 + half * HALF:rope0 + (half + 1) * HALF], (1, HEADS)))
    parts += [w[:, SCW:2 * SCW], w[:, 2 * SCW:3 * SCW], w[:, 0:SCW]]
    for i, t in enumerate(_tiles(np.concatenate(parts, 1), KT, 19)):
        put(BLOCK0["w_in"] + i, 0, t)
    uq = even_w_uq[0].reshape(QR, HEADS, QK)
    q_cols = [uq[:, :, NOPE:NOPE + HALF].reshape(QR, -1), uq[:, :, NOPE + HALF:].reshape(QR, -1),
              uq[:, :, :NOPE].reshape(QR, -1)]
    t = _tiles(np.concatenate(q_cols, 1), 3, 6)
    for i in range(6):
        put(BLOCK0["up_q"] + i // 2, 3 * (i % 2), t[i])
    ukv = even_w_ukv[0].reshape(KVR, HEADS, NOPE + DV)
    t = _tiles(ukv[:, :, :NOPE].reshape(KVR, -1), 2, 4)
    for i in range(4):
        put(BLOCK0["up_kn"], 2 * i, t[i])
    t = _tiles(ukv[:, :, NOPE:].reshape(KVR, -1), 2, 4)
    for k in range(2):
        put(BLOCK0["up_v"], 4 * k, t[:, k])
    for i, t in enumerate(_tiles(even_w_out[0], KT, KT)):
        put(BLOCK0["w_out"] + i, 0, t)
    for layer in range(2):
        up = _tiles(mlp_w1[layer], KT, FF // P)
        down = _tiles(mlp_w2[layer], FF // P, KT)
        for c in range(NCHUNK):
            for i in range(CHUNK):
                put(BLOCK0[f"mlp{layer}_up{c}"] + i, 0, up[c * CHUNK + i])
            for m in range(KT):
                for b in range(2):
                    k = c * CHUNK + b * SLOTS
                    put(BLOCK0[f"mlp{layer}_down{c}"] + 2 * m + b, 0, down[m, k:k + SLOTS])
    up = _tiles(odd_w_pw1[0], KT, 2 * KT)
    d = np.arange(P)
    for kind, j in PW1:
        n = BLOCK0["pw1"] + PW1_BLOCK[(kind, j)]
        if kind == "c":
            for t in range(PE_TAPS):
                out[n + t // SLOTS, d, t % SLOTS, d] = odd_w_dw[0, t, j * P:(j + 1) * P]
        else:
            put(n, 0, up[j + (KT if kind == "g" else 0)])
    for i, t in enumerate(_tiles(odd_w_pw2[0], KT, KT)):
        put(BLOCK0["pw2"] + i, 0, t)
    w = w_in_2[0]
    da = HEADS * HD
    q, k, v, fg, u = (w[:, 0:da], w[:, da:2 * da], w[:, 2 * da:3 * da], w[:, 3 * da:3 * da + HEADS], w[:, 3 * da + HEADS:])
    n0 = BLOCK0["w_in_2"]
    for i, t in enumerate(_tiles(q, KT, 4)):
        put(n0 + i, 0, t)
    put(n0 + 4, 0, _tiles(fg, KT, 1)[0])
    for i, t in enumerate(_tiles(u, KT, 4)):
        put(n0 + 5 + i, 0, t)
    t = _tiles(k, KT, 4)
    put(n0 + 9, 0, t[0])
    n0 = BLOCK0["w_in_2b"]
    for i in range(1, 4):
        put(n0 + i - 1, 0, t[i])
    t = _tiles(v, KT, 4)
    for k_tile in range(KT):
        put(n0 + 3 + k_tile // 2, 4 * (k_tile % 2), t[:, k_tile])
    put(BLOCK0["pool"], 0, w_pool_2[0])
    for i, t in enumerate(_tiles(w_out_2[0], KT, KT)):
        put(BLOCK0["w_out_2"] + i, 0, t)
    g, up = _tiles(w_gate_2[0], KT, HT2), _tiles(w_up_2[0], KT, HT2)
    for i in range(HT2):
        put(BLOCK0["ffn_up"] + 2 * i, 0, g[i])
        put(BLOCK0["ffn_up"] + 2 * i + 1, 0, up[i])
    down = _tiles(w_down_2[0], HT2, KT)
    for m in range(KT):
        for b in range(3):
            put(BLOCK0["ffn_down"] + 3 * m + b, 0, down[m, b * SLOTS:(b + 1) * SLOTS])
    return out


def _pack_vectors(v):
    out = np.zeros((P, NCOL), np.float32)

    def put(name, a, at=0):
        out[:a.shape[1], COL[name] + at:COL[name] + at + len(a)] = a.T

    put("gains", v["sandwich_gains"].reshape(-1, P))
    put("norm1_2", v["norm1_w_2"].reshape(-1, P))
    put("norm2_2", v["norm2_w_2"].reshape(-1, P))
    put("b_pw1", v["odd_b_pw1"].reshape(-1, P))
    put("w_dw", v["odd_w_dw"][0].reshape(TAPS, KT, P).transpose(1, 0, 2).reshape(-1, P))
    put("b_dw", v["odd_b_dw"].reshape(-1, P))
    put("ln_g", v["odd_ln_g"].reshape(-1, P))
    put("ln_b", v["odd_ln_b"].reshape(-1, P))
    put("b_pw2", v["odd_b_pw2"].reshape(-1, P))
    put("sc", v["even_sc_kernel"].reshape(-1, P))
    put("q_norm", v["even_q_norm"].reshape(-1, P))
    put("kv_norm", v["even_kv_norm"].reshape(-1, P))
    put("pool_scale", v["pool_scale_2"].reshape(-1, P))
    put("q_norm_2", np.tile(v["q_norm_w_2"], (1, 2)))
    put("k_norm_2", np.tile(v["k_norm_w_2"], (1, 2)))
    put("b_fgate", v["b_fgate_2"].reshape(1, -1))
    inv = np.float32(1) / np.power(np.float32(10000.0), np.arange(HALF, dtype=np.float32) / np.float32(HALF))
    put("inv_freq", np.tile(inv, P // HALF).reshape(1, P))
    return out


def kernel(**inputs):
    import concourse.bacc as bacc
    from concourse.bass_utils import run_bass_kernel_spmd

    v = {name: np.asarray(a) for name, a in inputs.items()}
    arrays = {
        "x_t": np.ascontiguousarray(v["x"][0].T.reshape(KT, P, S).transpose(1, 0, 2)),
        "meta_t": np.ascontiguousarray(v["meta_tokens_2"].T.reshape(KT, P, META).transpose(1, 0, 2)),
        "positions": np.ascontiguousarray(v["positions"]),
        "vectors": _pack_vectors(v),
        "weights": _pack_weights(*(v[n] for n in (
            "even_w_in", "even_w_uq", "even_w_ukv", "even_w_out", "mlp_w1", "mlp_w2", "odd_w_pw1", "odd_w_dw",
            "odd_w_pw2", "w_in_2", "w_pool_2", "w_out_2", "w_gate_2", "w_up_2", "w_down_2"))),
    }
    nc = bacc.Bacc("TRN2", target_bir_lowering=False, num_devices=1, dynamic_dma_scratch_size=1024)
    args = [nc.dram_tensor(name, a.shape, mybir.dt.from_np(a.dtype), kind="ExternalInput").ap()
            for name, a in arrays.items()]
    out = nc.dram_tensor("out_t", (P, KT, S), F32, kind="ExternalOutput").ap()
    build(nc, *args, out)
    r = run_bass_kernel_spmd(nc, [arrays], core_ids=[0])
    y = r.results[0]["out_t"]
    return np.ascontiguousarray(y.transpose(1, 0, 2).reshape(D, S).T)[None]
```
